# Optimizing a Trainium2 kernel written in Bass

```python
import jax, jax.numpy as jnp
from jax import lax
import numpy as np

D_MODEL = 1024
BATCH = 1
SEQ = 2048
DEPTH = 2

CHUNK = 64
N_MIXERS = 2
EPS = 1e-6

RET_HEADS = 4
RET_DK = D_MODEL // RET_HEADS
RET_DV = 2 * RET_DK
RET_QK_DIM = RET_HEADS * RET_DK
RET_V_DIM = RET_HEADS * RET_DV
RET_IN_DIM = 2 * RET_QK_DIM + 2 * RET_V_DIM
ROPE_BASE = 10000.0

POOL_WINDOWS = (2, 4, 8, 16)
POOL_GROUPS = len(POOL_WINDOWS)
POOL_GROUP_DIM = D_MODEL // POOL_GROUPS

MOE_GROUPS = 4
MOE_EXPERTS_PER_GROUP = 8
MOE_EXPERTS = MOE_GROUPS * MOE_EXPERTS_PER_GROUP
MOE_TOP_K = 2
MOE_D_FF = 256
MOE_BLOCK_ROWS = 128

kernel_name = "hybrid_retention_pool_hier_moe"

def rmsnorm(x, gain):
    xf = x.astype(jnp.float32)
    inv = lax.rsqrt(jnp.mean(xf * xf, axis=-1, keepdims=True) + EPS)
    return (xf * inv * gain.astype(jnp.float32)).astype(x.dtype)

def rope(x, pos):
    half = x.shape[-1] // 2
    inv_freq = 1.0 / (ROPE_BASE ** (jnp.arange(half, dtype=jnp.float32) / half))
    ang = pos[:, None] * inv_freq[None, :]
    cos = jnp.cos(ang)[None, :, None, :]
    sin = jnp.sin(ang)[None, :, None, :]
    x1, x2 = x[..., :half], x[..., half:]
    return jnp.concatenate([x1 * cos - x2 * sin, x1 * sin + x2 * cos], axis=-1)

def chunk_retention(q, k, v):
    B, H, S, dk = q.shape
    dv = v.shape[-1]
    n_chunks = S // CHUNK
    log_g = jnp.log(1.0 - jnp.exp2(-5.0 - jnp.arange(H, dtype=jnp.float32)))[:, None]
    j = jnp.arange(CHUNK, dtype=jnp.float32)
    intra_decay = jnp.exp(log_g[:, :, None] * jnp.abs(j[:, None] - j[None, :]))
    q_dec = jnp.exp(log_g * (j + 1.0))[None, :, :, None]
    k_dec = jnp.exp(log_g * (CHUNK - 1.0 - j))[None, :, :, None]
    chunk_dec = jnp.exp(log_g * CHUNK)[None, :, :, None]

    qc = q.reshape(B, H, n_chunks, CHUNK, dk)
    kc = k.reshape(B, H, n_chunks, CHUNK, dk)
    vc = v.reshape(B, H, n_chunks, CHUNK, dv)
    scores = jnp.einsum('bhncd,bhnmd->bhncm', qc, kc) * intra_decay[None, :, None]
    intra = jnp.einsum('bhncm,bhnme->bhnce', scores, vc)

    def step(state, inp):
        qn, kn, vn = inp
        cross = jnp.einsum('bhcd,bhde->bhce', qn * q_dec, state)
        state = state * chunk_dec + jnp.einsum('bhcd,bhce->bhde', kn * k_dec, vn)
        return state, cross

    xs = (jnp.moveaxis(qc, 2, 0), jnp.moveaxis(kc, 2, 0), jnp.moveaxis(vc, 2, 0))
    state0 = jnp.zeros((B, H, dk, dv), jnp.float32)
    _, cross = lax.scan(step, state0, xs)
    out = intra + jnp.moveaxis(cross, 0, 2)
    return out.reshape(B, H, S, dv)

def retention_mixer(h, w_in, w_out):
    B, S, _ = h.shape
    proj = h @ w_in
    q = proj[..., :RET_QK_DIM].astype(jnp.float32).reshape(B, S, RET_HEADS, RET_DK)
    k = proj[..., RET_QK_DIM:2 * RET_QK_DIM].astype(jnp.float32).reshape(B, S, RET_HEADS, RET_DK)
    v = proj[..., 2 * RET_QK_DIM:2 * RET_QK_DIM + RET_V_DIM].astype(jnp.float32).reshape(B, S, RET_HEADS, RET_DV)
    g = proj[..., 2 * RET_QK_DIM + RET_V_DIM:].astype(jnp.float32)
    pos = jnp.arange(S, dtype=jnp.float32)
    q = rope(q, pos)
    k = rope(k, pos) * (RET_DK ** -0.5)
    o = chunk_retention(q.transpose(0, 2, 1, 3), k.transpose(0, 2, 1, 3), v.transpose(0, 2, 1, 3))
    mu = jnp.mean(o, axis=-1, keepdims=True)
    var = jnp.mean(jnp.square(o - mu), axis=-1, keepdims=True)
    o = (o - mu) * lax.rsqrt(var + EPS)
    o = o.transpose(0, 2, 1, 3).reshape(B, S, RET_V_DIM)
    return (jax.nn.silu(g) * o).astype(h.dtype) @ w_out

def pool_mixer(h, w_group, scale):
    B, S, D = h.shape
    hg = h.astype(jnp.float32).reshape(B, S, POOL_GROUPS, POOL_GROUP_DIM)
    cs = jnp.concatenate([jnp.zeros((B, 1, POOL_GROUPS, POOL_GROUP_DIM), jnp.float32),
                          jnp.cumsum(hg, axis=1)], axis=1)
    t = jnp.arange(S)[:, None]
    win = jnp.array(POOL_WINDOWS, dtype=jnp.int32)[None, :]
    lo = jnp.maximum(t + 1 - win, 0)
    cnt = (t + 1 - lo).astype(jnp.float32)
    gidx = jnp.arange(POOL_GROUPS)[None, :]
    window_sum = cs[:, 1:] - cs[:, lo, gidx]
    pooled = window_sum / cnt[None, :, :, None] - hg
    y = jnp.einsum('bsgc,gcd->bsgd', pooled.astype(h.dtype), w_group).reshape(B, S, D)
    return y * scale

def hier_moe(h, w_group_router, b_group_router, w_expert_router, b_expert_router,
             w_gate, w_up, w_down):
    B, S, D = h.shape
    T = B * S
    xf = h.reshape(T, D)
    g_logits = (xf @ w_group_router).astype(jnp.float32) + b_group_router.astype(jnp.float32)
    g_prob = jax.nn.softmax(g_logits, axis=-1)
    grp = jnp.argmax(g_logits, axis=-1)
    g_gate = jnp.take_along_axis(g_prob, grp[:, None], axis=-1)
    e_logits = (xf @ w_expert_router).astype(jnp.float32).reshape(T, MOE_GROUPS, MOE_EXPERTS_PER_GROUP)
    e_logits = e_logits + b_expert_router.astype(jnp.float32)[None]
    e_sel = jnp.take_along_axis(e_logits, grp[:, None, None], axis=1)[:, 0]
    top_p, top_i = lax.top_k(jax.nn.softmax(e_sel, axis=-1), MOE_TOP_K)
    top_p = top_p / jnp.sum(top_p, axis=-1, keepdims=True)
    weights = g_gate * top_p
    expert = grp[:, None] * MOE_EXPERTS_PER_GROUP + top_i

    P = T * MOE_TOP_K
    n_blocks = -(-P // MOE_BLOCK_ROWS) + MOE_EXPERTS
    e_flat = expert.reshape(P)
    tok_flat = jnp.repeat(jnp.arange(T, dtype=jnp.int32), MOE_TOP_K)
    w_flat = weights.reshape(P)
    order = jnp.argsort(e_flat)
    e_s, tok_s, w_s = e_flat[order], tok_flat[order], w_flat[order]
    counts = jax.ops.segment_sum(jnp.ones((P,), jnp.int32), e_flat, num_segments=MOE_EXPERTS)
    starts = jnp.cumsum(counts) - counts
    padded = ((counts + MOE_BLOCK_ROWS - 1) // MOE_BLOCK_ROWS) * MOE_BLOCK_ROWS
    pad_ends = jnp.cumsum(padded)
    pad_starts = pad_ends - padded
    dest = pad_starts[e_s] + (jnp.arange(P, dtype=jnp.int32) - starts[e_s])
    buf_tok = jnp.full((n_blocks * MOE_BLOCK_ROWS,), T, jnp.int32).at[dest].set(tok_s)
    buf_w = jnp.zeros((n_blocks * MOE_BLOCK_ROWS,), jnp.float32).at[dest].set(w_s)
    blk_start = jnp.arange(n_blocks, dtype=jnp.int32) * MOE_BLOCK_ROWS
    blk_expert = jnp.minimum(jnp.searchsorted(pad_ends, blk_start, side='right'), MOE_EXPERTS - 1)
    x_pad = jnp.concatenate([xf, jnp.zeros((1, D), xf.dtype)], axis=0)

    def run_block(args):
        idx, e = args
        xb = x_pad[idx]
        hid = jax.nn.silu(xb @ w_gate[e]) * (xb @ w_up[e])
        return hid @ w_down[e]

    ys = lax.map(run_block, (buf_tok.reshape(n_blocks, MOE_BLOCK_ROWS), blk_expert))
    ys = ys * buf_w.reshape(n_blocks, MOE_BLOCK_ROWS, 1).astype(ys.dtype)
    out = jnp.zeros((T + 1, D), xf.dtype).at[buf_tok].add(ys.reshape(-1, D))[:T]
    return out.reshape(B, S, D)

def setup_inputs(seed: int = 0) -> dict:
    key = jax.random.key(seed)
    ks = jax.random.split(key, 16)
    n_ret = (DEPTH + N_MIXERS - 1) // N_MIXERS
    n_pool = DEPTH // N_MIXERS
    nrm = jax.random.normal
    x = nrm(ks[0], (BATCH, SEQ, D_MODEL), jnp.float32)
    norm_mix = 1.0 + 0.02 * nrm(ks[1], (DEPTH, D_MODEL), jnp.float32)
    norm_ffn = 1.0 + 0.02 * nrm(ks[2], (DEPTH, D_MODEL), jnp.float32)
    ret_w_in = nrm(ks[3], (n_ret, D_MODEL, RET_IN_DIM), jnp.float32) * D_MODEL ** -0.5
    ret_w_out = nrm(ks[4], (n_ret, RET_V_DIM, D_MODEL), jnp.float32) * RET_V_DIM ** -0.5
    pool_w = nrm(ks[5], (n_pool, POOL_GROUPS, POOL_GROUP_DIM, POOL_GROUP_DIM), jnp.float32) * POOL_GROUP_DIM ** -0.5
    pool_scale = 0.5 + 0.1 * nrm(ks[6], (n_pool, D_MODEL), jnp.float32)
    moe_w_group = nrm(ks[7], (DEPTH, D_MODEL, MOE_GROUPS), jnp.float32) * D_MODEL ** -0.5
    moe_b_group = 0.01 * nrm(ks[8], (DEPTH, MOE_GROUPS), jnp.float32)
    moe_w_expert = nrm(ks[9], (DEPTH, D_MODEL, MOE_EXPERTS), jnp.float32) * D_MODEL ** -0.5
    moe_b_expert = 0.01 * nrm(ks[10], (DEPTH, MOE_GROUPS, MOE_EXPERTS_PER_GROUP), jnp.float32)
    moe_w_gate = nrm(ks[11], (DEPTH, MOE_EXPERTS, D_MODEL, MOE_D_FF), jnp.float32) * D_MODEL ** -0.5
    moe_w_up = nrm(ks[12], (DEPTH, MOE_EXPERTS, D_MODEL, MOE_D_FF), jnp.float32) * D_MODEL ** -0.5
    moe_w_down = nrm(ks[13], (DEPTH, MOE_EXPERTS, MOE_D_FF, D_MODEL), jnp.float32) * MOE_D_FF ** -0.5
    final_norm = 1.0 + 0.02 * nrm(ks[14], (D_MODEL,), jnp.float32)
    return {"x": x, "norm_mix": norm_mix, "norm_ffn": norm_ffn,
            "ret_w_in": ret_w_in, "ret_w_out": ret_w_out,
            "pool_w": pool_w, "pool_scale": pool_scale,
            "moe_w_group": moe_w_group, "moe_b_group": moe_b_group,
            "moe_w_expert": moe_w_expert, "moe_b_expert": moe_b_expert,
            "moe_w_gate": moe_w_gate, "moe_w_up": moe_w_up, "moe_w_down": moe_w_down,
            "final_norm": final_norm}

def reference(x, norm_mix, norm_ffn, ret_w_in, ret_w_out, pool_w, pool_scale,
              moe_w_group, moe_b_group, moe_w_expert, moe_b_expert,
              moe_w_gate, moe_w_up, moe_w_down, final_norm):
    for layer in range(DEPTH):
        h = rmsnorm(x, norm_mix[layer])
        slot = layer // N_MIXERS
        if layer % N_MIXERS == 0:
            y = retention_mixer(h, ret_w_in[slot], ret_w_out[slot])
        else:
            y = pool_mixer(h, pool_w[slot], pool_scale[slot])
        x = x + y
        h = rmsnorm(x, norm_ffn[layer])
        x = x + hier_moe(h, moe_w_group[layer], moe_b_group[layer],
                         moe_w_expert[layer], moe_b_expert[layer],
                         moe_w_gate[layer], moe_w_up[layer], moe_w_down[layer])
    return rmsnorm(x, final_norm)


_drawn_inputs = setup_inputs


def setup_inputs(seed=0):
    import zlib

    import numpy as np

    out = dict(_drawn_inputs(seed))
    spreads = {}
    factors = {'moe_b_group': 3.237, 'moe_b_expert': 2.675, 'final_norm': 2.873}
    for name, (base, spread) in spreads.items():
        noise = np.random.default_rng([zlib.crc32(name.encode()), seed]).standard_normal(out[name].shape)
        drawn = base * np.exp(spread * noise) if base else spread * noise
        out[name] = __import__('jax').numpy.asarray(drawn.astype(out[name].dtype))
    for name, factor in factors.items():
        out[name] = (out[name] * factor).astype(out[name].dtype)
    return out
```

```python
from contextlib import ExitStack

import numpy as np
import concourse.bass as bass
from concourse import mybir

F32 = mybir.dt.float32
F32R = mybir.dt.float32r
I32 = mybir.dt.int32
ALU = mybir.AluOpType
ACT = mybir.ActivationFunctionType
AX = mybir.AxisListType

P = 128
SEQ = 2048
D = 1024
DC = D // P
TILES = SEQ // P
EPS = 1e-6

HEADS = 4
DK = D // HEADS
DV = 2 * DK
VDIM = HEADS * DV
VC = VDIM // P
CHUNK = 64
ROPE_BASE = 10000.0

WINDOWS = (2, 4, 8, 16)
PG = len(WINDOWS)
PGD = D // PG

GROUPS = 4
PER_GROUP = 8
EXPERTS = GROUPS * PER_GROUP
TOPK = 2
FF = 256
FC = FF // P
ROUTES = GROUPS + EXPERTS
BLOCKS = SEQ * TOPK // P + EXPERTS
BIG = 1e30


def ds(start, size):
    return bass.ds(start, size)


def three_pass(pe, out, x_hi, x_lo, w_hi, w_lo, first, last):
    pe.matmul(out, x_hi, w_hi, start=first, stop=False)
    pe.matmul(out, x_hi, w_lo, start=False, stop=False)
    return pe.matmul(out, x_lo, w_hi, start=False, stop=last)


def skewed(eng, n, front, back):
    front(0, 0)
    with eng.Fori(0, n // 2 - 1) as i:
        front(2 * i + 1, 1)
        back(2 * i, 0)
        front(2 * i + 2, 0)
        back(2 * i + 1, 1)
    front(n - 1, 1)
    back(n - 2, 0)
    back(n - 1, 1)


def pairs(eng, n, step):
    with eng.Fori(0, n // 2) as i:
        step(2 * i, 0)
        step(2 * i + 1, 1)


class Scope:

    def __init__(self, nc, tag, past):
        self.nc, self.tag, self.ctx, self.ticks = nc, tag, ExitStack(), {}
        self.sems, self.past = [], past

    def __enter__(self):
        self.ctx.__enter__()
        return self

    def __exit__(self, *a):
        self.ctx.__exit__(*a)
        if self.past:
            for sem in self.past[-1].sems:
                self.nc.release_semaphore(sem)
        self.past.append(self)

    def clear_before(self, eng):
        for sem in self.past[-1].sems:
            eng.sem_clear(sem)

    def sb(self, name, shape, dt=F32):
        return self.ctx.enter_context(self.nc.sbuf_tensor(f"{self.tag}_{name}", shape, dt))

    def slots(self, name, n, shape, dt=F32):
        t = self.sb(name, [shape[0], n] + shape[1:], dt)
        return [t[:, i] for i in range(n)]

    def ps(self, name, shape, dt=F32):
        return self.ctx.enter_context(self.nc.psum_tensor(f"{self.tag}_{name}", shape, dt))

    def sem(self, name):
        self.sems.append(self.nc.alloc_semaphore(f"{self.tag}_{name}"))
        return self.sems[-1]

    def passed(self, eng):
        eng.sem_inc(self.ticks[eng.engine], 1)

    def block(self):
        for name in ("PE", "DVE", "Activation", "Pool", "SP"):
            self.ticks[mybir.EngineType[name]] = self.sem(f"passed_{name}")
        return self.ctx.enter_context(self.nc.Block())



def moe_phase(nc, past, tag, h, w_gate, w_up, w_down, y_rows, token_of_row, block_of_expert, ident):
    with Scope(nc, tag, past) as s:
        raw_gate = s.slots("raw_gate", 2, [P, DC, FF])
        raw_up = s.slots("raw_up", 2, [P, DC, FF])
        raw_down = s.slots("raw_down", 2, [P, FC, D])
        gu_hi = s.slots("gu_hi", 2, [P, DC, 2 * FF], F32R)
        gu_lo = s.slots("gu_lo", 2, [P, DC, 2 * FF], F32R)
        dn_hi = s.slots("dn_hi", 2, [P, FC, D], F32R)
        dn_lo = s.slots("dn_lo", 2, [P, FC, D], F32R)
        rows = s.sb("rows", [P, D])
        row_index = s.sb("row_index", [P, 1], I32)
        x_hi = s.sb("x_hi", [P, DC, P], F32R)
        x_lo = s.sb("x_lo", [P, DC, P], F32R)
        silu = s.sb("silu", [P, FC, P])
        hid = s.sb("hid", [P, FC, P])
        hT_hi = s.sb("hT_hi", [P, FC, P], F32R)
        hT_lo = s.sb("hT_lo", [P, FC, P], F32R)
        y = s.sb("y", [P, 2, D])

        ps_x = s.ps("ps_x", [P, DC, P])
        ps_gu = [s.ps(f"ps_gu{j}", [P, 4, P]) for j in range(FC)]
        ps_hT = [s.ps(f"ps_hT{j}", [P, 512]) for j in range(FC)]
        ps_y = s.ps("ps_y", [P, D])

        warm = s.sb("warm", [P, 1])
        ones_set = s.sem("ones_set")
        warmed = s.sem("warmed")
        gate_landed = [s.sem(f"gate_landed{i}") for i in range(2)]
        up_landed = [s.sem(f"up_landed{i}") for i in range(2)]
        down_landed = [s.sem(f"down_landed{i}") for i in range(2)]
        w_hi_ready = s.sem("w_hi_ready")
        gu_split = s.sem("gu_split")
        dn_split = s.sem("dn_split")
        index_ready = s.sem("index_ready")
        rows_landed = s.sem("rows_landed")
        xT_ready = s.sem("xT_ready")
        x_hi_ready = s.sem("x_hi_ready")
        x_split = s.sem("x_split")
        gu_ready = s.sem("gu_ready")
        silu_ready = s.sem("silu_ready")
        hid_ready = s.sem("hid_ready")
        hT_ready = s.sem("hT_ready")
        hT_hi_ready = s.sem("hT_hi_ready")
        hT_split = s.sem("hT_split")
        y_summed = s.sem("y_summed")
        y_left = s.sem("y_left")
        y_right = s.sem("y_right")
        y_stored = s.sem("y_stored")
        y_free = s.sem("y_free")

        CHUNKS = 6
        HI_ORDER = (4, 0, 5, 1, 2, 3)

        def chunk(buf, par, k):
            if k < 4:
                half, up = k // 2, k % 2
                c = slice(half * DC // 2, (half + 1) * DC // 2)
                if buf is None:
                    return (raw_up if up else raw_gate)[par][:, c, :]
                return buf[0][par][:, c, up * FF:(up + 1) * FF]
            if buf is None:
                return raw_down[par][:, k - 4, :]
            return buf[1][par][:, k - 4, :]

        HI, LO = (gu_hi, dn_hi), (gu_lo, dn_lo)
        landed = [gate_landed, up_landed, gate_landed, up_landed, down_landed, down_landed]

        def over_blocks(eng, e, first_step, step, ready=None):
            b0 = eng.value_load(block_of_expert[0:1, ds(e, 1)], min_val=0, max_val=BLOCKS - 1)
            b1 = eng.value_load(block_of_expert[0:1, ds(e + 1, 1)], min_val=1, max_val=BLOCKS)
            if ready:
                eng.wait_ge(*ready)
            first_step(b0)
            with eng.If(b1 > b0 + 1):
                with eng.Fori(b0 + 1, b1) as b:
                    step(b)

        def over_experts(eng, body):
            with eng.Fori(0, EXPERTS // 2 - 1) as i:
                body(2 * i, 0, True)
                body(2 * i + 1, 1, True)
            body(EXPERTS - 2, 0, True)
            body(EXPERTS - 1, 1, False)

        blk = s.block()

        @blk.sync
        def _(sp):
            def load(e, par, wait):
                if wait:
                    sp.wait_ge(gu_split, 4 * (e - 1))
                sp.dma_start(raw_gate[par][:, :, :], w_gate[e].rearrange("(c p) f -> p c f", p=P)
                             ).then_inc(gate_landed[par], 16)
                sp.dma_start(raw_up[par][:, :, :], w_up[e].rearrange("(c p) f -> p c f", p=P)
                             ).then_inc(up_landed[par], 16)
                if wait:
                    sp.wait_ge(dn_split, 2 * (e - 1))
                sp.dma_start(raw_down[par][:, :, :], w_down[e].rearrange("(c p) d -> p c d", p=P)
                             ).then_inc(down_landed[par], 16)
            load(0, 0, False)
            load(1, 1, False)
            with sp.Fori(1, EXPERTS // 2) as i:
                load(2 * i, 0, True)
                load(2 * i + 1, 1, True)

        @blk.gpsimd
        def _(pool):
            pool.memset(warm[:, :], 1.0).then_inc(ones_set, 1)
            s.clear_before(pool)
            def gather(b):
                if not (isinstance(b, int) and b == 0):
                    pool.wait_ge(xT_ready, 2 * b)
                pool.tensor_copy(row_index[:, :], token_of_row[:, ds(b, 1)]).then_inc(index_ready, 1)
                pool.wait_ge(index_ready, 1)
                pool.sem_clear(index_ready)
                pool.indirect_dma_start(
                    out=rows[:, :], out_offset=None, in_=h[:, :],
                    in_offset=bass.IndirectOffsetOnAxis(ap=row_index[:, 0:1], axis=0),
                ).then_inc(rows_landed, 16)

            def split_down(e, par):
                for k in (4, 5):
                    pool.wait_ge(w_hi_ready, CHUNKS * e + HI_ORDER.index(k) + 1)
                    pool.tensor_tensor(chunk(LO, par, k), chunk(None, par, k),
                                       chunk(HI, par, k).bitcast(F32), ALU.subtract).then_inc(dn_split, 1)

            def step(b, fill=lambda: None):
                gather(b + 2)
                fill()
                pool.wait_ge(y_left, b + 1)
                pool.wait_ge(y_right, b + 1)
                pool.wait_ge(y_stored, 16 * b)
                pool.sem_inc(y_free, 1)
                pool.dma_start(y_rows[ds(b * P, P), :], y[:, ds(b % 2, 1), :].rearrange("p a d -> p (a d)")
                               ).then_inc(y_stored, 16)

            gather(0)
            gather(1)
            pool.sem_inc(y_free, 1)
            split_down(0, 0)

            def expert(e, par, more):
                over_blocks(pool, e, lambda b: step(b, (lambda: split_down(e + 1, 1 - par)) if more else lambda: None), step)
            over_experts(pool, expert)
            total = pool.value_load(block_of_expert[0:1, EXPERTS:EXPERTS + 1], min_val=1, max_val=BLOCKS)
            pool.wait_ge(y_stored, 16 * total)
            pool.wait_ge(rows_landed, 16 * (total + 2))

        @blk.scalar
        def _(act):
            def split_w(e, pair, par, k):
                act.wait_ge(landed[k][par], 16 * (pair + 1))
                act.activation(chunk(HI, par, k), chunk(None, par, k), ACT.Copy).then_inc(w_hi_ready, 1)

            def split_x(b, j):
                act.wait_ge(xT_ready, 2 * b + j + 1)
                c = slice(4 * j, 4 * j + 4)
                act.activation(x_hi[:, c, :], ps_x[:, c, :], ACT.Copy).then_inc(x_hi_ready, 1)

            def block(b, fill):
                for j in range(FC):
                    fill(HI_ORDER[2 * j])
                    fill(HI_ORDER[2 * j + 1])
                    act.wait_ge(gu_ready, 2 * b + j + 1)
                    act.activation(silu[:, j, :], ps_gu[j][:, 0, :], ACT.Silu).then_inc(silu_ready, 1)
                for j in range(FC):
                    act.wait_ge(hT_ready, 2 * b + j + 1)
                    act.activation(hT_hi[:, j, :], ps_hT[j][:, 0:P], ACT.Copy).then_inc(hT_hi_ready, 1)
                    split_x(b + 1, j)
                for k in HI_ORDER[4:]:
                    fill(k)
                act.wait_ge(y_summed, 2 * b + 1)
                act.wait_ge(y_free, b + 1)
                s.passed(act)
                act.activation(y[:, ds(b % 2, 1), 0:D // 2].rearrange("p a d -> p (a d)"), ps_y[:, 0:D // 2], ACT.Copy).then_inc(y_left, 1)

            def expert(e, par, more):
                def first(b):
                    if more:
                        act.wait_ge(y_summed, 2 * b)
                        pair = (e + 1) // 2 if isinstance(e, int) else (e + 1 - (1 - par)) // 2
                        block(b, lambda k: split_w(e + 1, pair, 1 - par, k))
                    else:
                        block(b, lambda k: None)
                over_blocks(act, e, first, lambda b: block(b, lambda k: None))

            act.wait_ge(ones_set, 1)
            act.activation(warm[:, :], warm[:, :], ACT.Silu).then_inc(warmed, 1)
            for k in HI_ORDER:
                split_w(0, 0, 0, k)
            for j in range(2):
                split_x(0, j)
            over_experts(act, expert)

        @blk.vector
        def _(dve):
            def split_w(e, par, k):
                dve.wait_ge(w_hi_ready, CHUNKS * e + HI_ORDER.index(k) + 1)
                dve.tensor_tensor(chunk(LO, par, k), chunk(None, par, k),
                                  chunk(HI, par, k).bitcast(F32), ALU.subtract).then_inc(gu_split, 1)

            def split_x(b, j):
                c = slice(4 * j, 4 * j + 4)
                dve.wait_ge(x_hi_ready, 2 * b + j + 1)
                dve.tensor_tensor(x_lo[:, c, :], ps_x[:, c, :], x_hi[:, c, :].bitcast(F32),
                                  ALU.subtract).then_inc(x_split, 1)

            def block(b, fill):
                for j in range(FC):
                    fill(j)
                    dve.wait_ge(silu_ready, 2 * b + j + 1)
                    dve.tensor_tensor(hid[:, j, :], silu[:, j, :], ps_gu[j][:, 1, :], ALU.mult).then_inc(hid_ready, 1)
                for j in range(FC):
                    dve.wait_ge(hT_hi_ready, 2 * b + j + 1)
                    dve.tensor_tensor(hT_lo[:, j, :], ps_hT[j][:, 0:P], hT_hi[:, j, :].bitcast(F32),
                                      ALU.subtract).then_inc(hT_split, 1)
                    split_x(b + 1, j)
                for k in range(2, 4):
                    fill(k)
                dve.wait_ge(y_summed, 2 * b + 2)
                dve.wait_ge(y_free, b + 1)
                s.passed(dve)
                dve.tensor_copy(y[:, ds(b % 2, 1), D // 2:D].rearrange("p a d -> p (a d)"), ps_y[:, D // 2:D]).then_inc(y_right, 1)

            def expert(e, par, more):
                if more:
                    first = lambda b: block(b, lambda k: split_w(e + 1, 1 - par, k))
                else:
                    first = lambda b: block(b, lambda k: None)
                over_blocks(dve, e, first, lambda b: block(b, lambda k: None))

            for k in range(4):
                split_w(0, 0, k)
            for j in range(2):
                split_x(0, j)
            over_experts(dve, expert)

        @blk.tensor
        def _(pe):
            def transpose_rows(b):
                pe.wait_ge(rows_landed, 16 * (b + 1))
                for j in range(2):
                    for c in range(4 * j, 4 * j + 4):
                        last = pe.transpose(ps_x[:, c, :], rows[:, c * P:(c + 1) * P], ident[:, :])
                    last.then_inc(xT_ready, 1)

            def block(e, par, b):
                pe.wait_ge(x_split, 2 * b + 2)
                for j in range(FC):
                    for c in range(DC):
                        units = [w[par][:, c, :].rearrange("p (a j n) -> p j a n", a=2, j=FC)[:, j]
                                 for w in (gu_hi, gu_lo)]
                        last = three_pass(pe, ps_gu[j][:, 0:2, :], x_hi[:, c, :], x_lo[:, c, :],
                                          *units, c == 0, c == DC - 1)
                    last.then_inc(gu_ready, 1)
                for j in range(FC):
                    pe.wait_ge(hid_ready, 2 * b + j + 1)
                    pe.transpose(ps_hT[j][:, 0:P], hid[:, j, :], ident[:, :]).then_inc(hT_ready, 1)
                    if j == 0:
                        transpose_rows(b + 1)
                pe.wait_ge(dn_split, 2 * (e + 1))
                pe.wait_ge(y_left, b)
                pe.wait_ge(y_right, b)
                for c in range(FC):
                    pe.wait_ge(hT_split, 2 * b + c + 1)
                    for n in range(2):
                        cols = slice(n * D // 2, (n + 1) * D // 2)
                        last = three_pass(pe, ps_y[:, cols], hT_hi[:, c, :], hT_lo[:, c, :],
                                          dn_hi[par][:, c, cols], dn_lo[par][:, c, cols], c == 0, c == FC - 1)
                        if c == FC - 1:
                            last.then_inc(y_summed, 1)

            def expert(e, par, more):
                over_blocks(pe, e, lambda b: block(e, par, b), lambda b: block(e, par, b),
                            ready=(gu_split, 4 * (e + 1)))

            transpose_rows(0)
            over_experts(pe, expert)



def norm_transpose_phase(nc, past, x, gain, hT, ident, ident_table):
    with Scope(nc, "norm0", past) as s:
        gain_b = s.sb("gain_b", [P, D])
        x_in = s.slots("x_in", 2, [P, D])
        square = s.sb("square", [P, D])
        sumsq = s.slots("sumsq", 2, [P, 1])
        mean_eps = s.slots("mean_eps", 2, [P, 1])
        power = s.sb("power", [P, 1])
        rstd = s.slots("rstd", 2, [P, 1])
        hn = s.slots("hn", 2, [P, D])
        ps_t = [s.ps(f"ps_t{i}", [P, DC, P]) for i in range(2)]

        ident_landed = s.sem("ident_landed")
        gain_landed = s.sem("gain_landed")
        x_landed = [s.sem(f"x_landed{i}") for i in range(2)]
        power_set = s.sem("power_set")
        sumsq_ready = s.sem("sumsq_ready")
        mean_ready = s.sem("mean_ready")
        rstd_ready = s.sem("rstd_ready")
        hn_ready = s.sem("hn_ready")
        transposed = s.sem("transposed")
        left_copied = s.sem("left_copied")
        right_copied = s.sem("right_copied")
        blk = s.block()
        H = DC // 2

        @blk.sync
        def _(sp):
            sp.dma_start(gain_b[:, :], gain.rearrange("(a d) -> a d", a=1).to_broadcast([P, D])
                         ).then_inc(gain_landed, 16)

            def load(t, par):
                if not isinstance(t, int) or t >= 2:
                    sp.wait_ge(hn_ready, t - 1)
                sp.dma_start(x_in[par][:, :], x[ds(t * P, P), :]).then_inc(x_landed[par], 16)
            load(0, 0)
            load(1, 1)
            sp.dma_start(ident[:, :], ident_table).then_inc(ident_landed, 16)
            with sp.Fori(1, TILES // 2) as i:
                load(2 * i, 0)
                load(2 * i + 1, 1)

        @blk.gpsimd
        def _(pool):
            pool.memset(power[:, :], -0.5).then_inc(power_set, 1)
            pool.wait_ge(power_set, 1)

            def step(t, par):
                pool.wait_ge(sumsq_ready, t + 1)
                s.passed(pool)
                pool.tensor_scalar(mean_eps[par][:, :], sumsq[par][:, :], 1.0 / D, EPS,
                                   ALU.mult, ALU.add).then_inc(mean_ready, 1)
                pool.wait_ge(mean_ready, t + 1)
                pool.tensor_tensor(rstd[par][:, :], mean_eps[par][:, :], power[:, :],
                                   ALU.pow).then_inc(rstd_ready, 1)
            pairs(pool, TILES, step)

        @blk.scalar
        def _(act):
            def front(t, par):
                act.wait_ge(x_landed[par], 8 * (t - par) + 16)
                act.wait_ge(sumsq_ready, t)
                if not isinstance(t, int) or t >= 2:
                    act.wait_ge(rstd_ready, t - 1)
                act.activation(square[:, :], x_in[par][:, :], ACT.Square,
                               accum_out=sumsq[par][:, :]).then_inc(sumsq_ready, 1)

            def back(t, par):
                act.wait_ge(transposed, t + 1)
                s.passed(act)
                act.activation(hT[:, 0:H, ds(t * P, P)], ps_t[par][:, 0:H, :], ACT.Copy).then_inc(left_copied, 1)
            skewed(act, TILES, front, back)

        @blk.vector
        def _(dve):
            dve.wait_ge(gain_landed, 16)

            def front(t, par):
                dve.wait_ge(rstd_ready, t + 1)
                if not isinstance(t, int) or t >= 2:
                    dve.wait_ge(transposed, t - 1)
                dve.scalar_tensor_tensor(out=hn[par][:, :], in0=x_in[par][:, :], scalar=rstd[par][:, 0:1],
                                         in1=gain_b[:, :], op0=ALU.mult, op1=ALU.mult).then_inc(hn_ready, 1)

            def back(t, par):
                dve.wait_ge(transposed, t + 1)
                dve.tensor_copy(hT[:, H:DC, ds(t * P, P)], ps_t[par][:, H:DC, :]).then_inc(right_copied, 1)
            skewed(dve, TILES, front, back)

        @blk.tensor
        def _(pe):
            def step(t, par):
                pe.wait_ge(hn_ready, t + 1)
                if not isinstance(t, int) or t >= 2:
                    pe.wait_ge(left_copied, t - 1)
                    pe.wait_ge(right_copied, t - 1)
                for c in range(DC):
                    last = pe.transpose(ps_t[par][:, c, :], hn[par][:, c * P:(c + 1) * P], ident[:, :])
                last.then_inc(transposed, 1)
            pe.wait_ge(ident_landed, 16)
            step(0, 0)
            step(1, 1)
            with pe.Fori(1, TILES // 2) as i:
                step(2 * i, 0)
                step(2 * i + 1, 1)


def retention_phase(nc, past, hT, w_in, rope, decay, mask, qk_rows, gate_rows, y_rows, ident, expert_rows):
    with Scope(nc, "ret", past) as s:
        raw = s.sb("raw", [P, DC, 512])
        w_hi = s.slots("w_hi", 2, [P, DC, 512], F32R)
        w_lo = s.slots("w_lo", 2, [P, DC, 512], F32R)
        x_hi = s.slots("x_hi", 2, [P, DC, P], F32R)
        x_lo = s.slots("x_lo", 2, [P, DC, P], F32R)
        gate = s.slots("gate", 2, [P, DV])
        rope_in = s.slots("rope_in", 2, [P, 3, P])
        qk_dec = s.sb("qk_dec", [P, 2, 2, P])
        sin_part = s.sb("sin_part", [P, 2, 2, P])
        qk_out = s.slots("qk_out", 2, [P, 2, 2, P])
        qk_in = s.slots("qk_in", 2, [P, 4, P])
        qkT = s.sb("qkT", [P, 4, P])
        value = s.sb("value", [P, DV])
        scores = s.sb("scores", [P, P])
        state = s.sb("state", [P, 2, DV])
        stats = s.sb("stats", [P, 6])
        mean_var = s.sb("mean_var", [P, 2])
        var_eps = s.sb("var_eps", [P, 1])
        power = s.sb("power", [P, 1])
        rstd = s.sb("rstd", [P, 1])
        normed = s.sb("normed", [P, DV])
        y_out = s.slots("y_out", 2, [P, DV])
        decay_sb = s.sb("decay_sb", [P, 3 * HEADS])
        mask_sb = s.sb("mask_sb", [P, HEADS, P])
        zeros = s.sb("zeros", [P, 512])
        warm = s.sb("warm", [P, 1])

        ps_p = [s.ps(f"ps_p{i}", [P, 512]) for i in range(2)]
        ps_t = s.ps("ps_t", [P, 4, P])
        ps_s = s.ps("ps_s", [P, 512])
        ps_o = s.ps("ps_o", [P, DV])
        ps_state = s.ps("ps_state", [P, 2, DV])

        consts_landed = s.sem("consts_landed")
        raw_landed = [s.sem(f"raw_landed{i}") for i in range(2)]
        w_hi_ready = s.sem("w_hi_ready")
        w_split = s.sem("w_split")
        x_hi_ready = s.sem("x_hi_ready")
        x_split = s.sem("x_split")
        projected = s.sem("projected")
        consumed = s.sem("consumed")
        gate_stored = [s.sem(f"gate_stored{i}") for i in range(2)]
        rope_landed = [s.sem(f"rope_landed{i}") for i in range(2)]
        rope_parts = s.sem("rope_parts")
        roped = s.sem("roped")
        qk_stored = [s.sem(f"qk_stored{i}") for i in range(2)]
        qk_landed = [s.sem(f"qk_landed{i}") for i in range(2)]
        gate_landed = [s.sem(f"gate_landed{i}") for i in range(2)]
        qk_transposed = s.sem("qk_transposed")
        qkT_ready = s.sem("qkT_ready")
        scored = s.sem("scored")
        masked = s.sem("masked")
        mixed = s.sem("mixed")
        outer_ready = s.sem("outer_ready")
        state_ready = s.sem("state_ready")
        stats_ready = s.sem("stats_ready")
        mean_ready = s.sem("mean_ready")
        var_ready = s.sem("var_ready")
        power_set = s.sem("power_set")
        rstd_ready = s.sem("rstd_ready")
        normed_ready = s.sem("normed_ready")
        y_ready = s.sem("y_ready")
        y_stored = [s.sem(f"y_stored{i}") for i in range(2)]
        zeros_set = s.sem("zeros_set")
        zeros_stored = s.sem("zeros_stored")
        blk = s.block()

        T = TILES
        FIRST_SPARE = SEQ * TOPK
        ZR = (BLOCKS * P - FIRST_SPARE) // (HEADS * T)
        QK, GATE, VALUE = KINDS = range(3)
        HB = (T // 2) // 2

        def passes(eng, body):
            with eng.Fori(0, HEADS // 2) as hp:
                for hh in range(2):
                    for kind in KINDS:
                        after = 2 * hp + 1 if hh == 0 else 2 - 2 * hp
                        body(kind, 2 * hp + hh, 6 * hp + 3 * hh + kind, (3 * hh + kind) % 2, after)

        def over_tiles(eng, tile, half):
            with eng.Fori(0, HB) as i:
                tile(2 * i, 0, i, True)
                tile(2 * i + 1, 1, i, True)
            half(0)
            with eng.Fori(HB, T // 2 - 1) as i:
                tile(2 * i, 0, i, True)
                tile(2 * i + 1, 1, i, True)
            tile(T - 2, 0, T // 2 - 1, False)
            tile(T - 1, 1, T // 2 - 1, False)
            half(1)

        @blk.sync
        def _(sp):
            sp.dma_start(decay_sb[:, :], decay).then_inc(consts_landed, 16)
            sp.dma_start(mask_sb[:, :, :], mask).then_inc(consts_landed, 16)

            def load_half(kind, h, j):
                rows = w_in[j * (D // 2):(j + 1) * (D // 2), :].rearrange("(c p) n -> p c n", p=P)
                c = slice(4 * j, 4 * j + 4)
                if kind == QK:
                    sp.dma_start(raw[:, c, 0:DK], rows[:, :, ds(h * DK, DK)]).then_inc(raw_landed[j], 16)
                    sp.dma_start(raw[:, c, DK:2 * DK], rows[:, :, ds(D + h * DK, DK)]).then_inc(raw_landed[j], 16)
                else:
                    base = 2 * D + (VDIM if kind == GATE else 0)
                    sp.dma_start(raw[:, c, :], rows[:, :, ds(base + h * DV, DV)]).then_inc(raw_landed[j], 32)

            def load_rope(t, par, used):
                if used is not None:
                    sp.wait_ge(rope_parts, used)
                sp.dma_start(rope_in[par][:, :, :], rope[ds(t * P, P), :].rearrange("p (a d) -> p a d", a=3)
                             ).then_inc(rope_landed[par], 16)

            load_half(QK, 0, 0)
            load_half(QK, 0, 1)
            sp.wait_ge(zeros_set, 1)
            for j in range(2):
                sp.wait_ge(w_split, 8 * (j + 1))
                load_half(GATE, 0, j)
            load_rope(0, 0, None)
            load_rope(1, 1, None)

            def one_pass(kind, h, p, slot, after):
                def half(j):
                    sp.wait_ge(w_split, T * (p + 1) + 8 * (j + 1))
                    s.passed(sp)
                    load_half((kind + 2) % 3, h if kind == QK else after, j)
                    s.passed(sp)

                def load_qk(t, par):
                    g = h * T + t
                    sp.dma_start(qk_in[par][:, :, :].rearrange("p a d -> p (a d)"),
                                 qk_rows[ds(g * P, P), :]).then_inc(qk_landed[par], 16)

                def load_gate(t, par):
                    g = h * T + t
                    sp.dma_start(gate[par][:, :], gate_rows[ds(g * P, P), :]).then_inc(gate_landed[par], 16)

                def tile(t, par, i, more):
                    g, G = h * T + t, p * T + t
                    if kind == GATE:
                        sp.wait_ge(consumed, G + 2)
                        sp.dma_start(gate_rows[ds(g * P, P), :], gate[par][:, :]).then_inc(gate_stored[par], 16)
                    elif kind == QK:
                        sp.wait_ge(roped, g + 1)
                        sp.dma_start(qk_rows[ds(g * P, P), :], qk_out[par][:, :, :, :].rearrange(
                            "p a b d -> p (a b d)")).then_inc(qk_stored[par], 16)
                        load_rope(t + 2 if more else par, par, 3 * (g + 1))
                    else:
                        sp.wait_ge(y_ready, g + 1)
                        sp.dma_start(y_rows[ds(t * P, P), ds(h * DV, DV)], y_out[par][:, :]).then_inc(y_stored[par], 16)
                        sp.dma_start(expert_rows[ds(FIRST_SPARE + g * ZR, ZR), :].rearrange("r (a n) -> (r a) n", a=2),
                                     zeros[0:2 * ZR, :]).then_inc(zeros_stored, 16)
                        if more:
                            sp.wait_ge(outer_ready, g + 1)
                            load_qk(t + 2, par)
                            load_gate(t + 2, par)

                if kind == GATE:
                    for i in range(2):
                        sp.wait_ge(qk_stored[i], 8 * T * (h + 1))
                    sp.wait_ge(outer_ready, T * h)
                    load_qk(0, 0)
                    load_qk(1, 1)
                if kind == VALUE:
                    for i in range(2):
                        sp.wait_ge(gate_stored[i], 8 * T * (h + 1))
                    s.passed(sp)
                    load_gate(0, 0)
                    load_gate(1, 1)
                over_tiles(sp, tile, half)
            passes(sp, one_pass)
            for i in range(2):
                sp.wait_ge(y_stored[i], 8 * T * HEADS)
                sp.wait_ge(rope_landed[i], 8 * T * HEADS + 16)
                sp.wait_ge(raw_landed[i], 32 * (3 * HEADS + 2))
            sp.wait_ge(zeros_stored, 16 * T * HEADS)

        @blk.gpsimd
        def _(pool):
            s.clear_before(pool)
            pool.memset(zeros[:, :], 0.0).then_inc(zeros_set, 1)
            pool.memset(power[:, :], -0.5).then_inc(power_set, 1)
            pool.wait_ge(power_set, 1)
            with pool.Fori(0, HEADS * T) as g:
                pool.wait_ge(mean_ready, g + 1)
                s.passed(pool)
                pool.tensor_scalar(var_eps[:, :], mean_var[:, 1:2], 1.0, EPS, ALU.mult, ALU.add).then_inc(var_ready, 1)
                pool.wait_ge(var_ready, g + 1)
                pool.tensor_tensor(rstd[:, :], var_eps[:, :], power[:, :], ALU.pow).then_inc(rstd_ready, 1)

        def w_chunk(buf, i, par):
            return buf[:, ds(i, 1), par * 256:(par + 1) * 256]

        @blk.scalar
        def _(act):
            act.wait_ge(power_set, 1)
            act.activation(warm[:, :], power[:, :], ACT.Silu).then_inc(consumed, 1)
            act.wait_ge(consts_landed, 32)

            def split_w(slot, i, par):
                act.activation(w_chunk(w_hi[slot], i, par), w_chunk(raw, i, par), ACT.Copy).then_inc(w_hi_ready, 1)

            def split_x(t, par):
                act.activation(x_hi[par][:, :, :], hT[:, :, ds(t * P, P)], ACT.Copy).then_inc(x_hi_ready, 1)

            for j in range(2):
                act.wait_ge(raw_landed[j], 32)
                with act.Fori(4 * j, 4 * j + 4) as i:
                    split_w(0, i, 0)
                    split_w(0, i, 1)
            split_x(0, 0)

            def one_pass(kind, h, p, slot, after):
                def tile(t, par, i, more):
                    g, G = h * T + t, p * T + t
                    act.wait_ge(projected, G)
                    s.passed(act)
                    split_x(0 if isinstance(t, int) and t == T - 1 else t + 1, 1 - par)
                    split_w(1 - slot, i, par)
                    if kind == VALUE:
                        act.wait_ge(qk_transposed, g + 1)
                        act.wait_ge(mixed, g)
                        act.activation(qkT[:, :, :], ps_t[:, :, :], ACT.Copy).then_inc(qkT_ready, 1)
                    act.wait_ge(projected, G + 1)
                    if kind == GATE:
                        act.wait_ge(gate_stored[par], 8 * (g - par))
                        act.activation(gate[par][:, :], ps_p[par][:, :], ACT.Silu).then_inc(consumed, 1)
                    elif kind == QK:
                        act.wait_ge(rope_parts, 3 * g)
                        s.passed(act)
                        act.activation(qk_dec[:, 0, :, :].rearrange("p b d -> p (b d)"), ps_p[par][:, 0:DK],
                                       ACT.Copy, scale=decay_sb[:, ds(3 * h, 1)])
                        act.activation(qk_dec[:, 1, :, :].rearrange("p b d -> p (b d)"), ps_p[par][:, DK:2 * DK],
                                       ACT.Copy, scale=decay_sb[:, ds(3 * h + 1, 1)]).then_inc(consumed, 1)
                    else:
                        act.wait_ge(outer_ready, g)
                        act.activation(value[:, :], ps_p[par][:, :], ACT.Copy).then_inc(consumed, 1)

                def half(j):
                    if j == 0:
                        act.wait_ge(raw_landed[1], 32 * (p + 2))

                if kind == GATE:
                    act.wait_ge(y_ready, T * h)
                act.wait_ge(raw_landed[0], 32 * (p + 2))
                over_tiles(act, tile, half)
            passes(act, one_pass)

        @blk.vector
        def _(dve):
            dve.wait_ge(consts_landed, 32)

            def split_w(slot, i, par):
                dve.tensor_tensor(w_chunk(w_lo[slot], i, par), w_chunk(raw, i, par),
                                  w_chunk(w_hi[slot], i, par).bitcast(F32), ALU.subtract).then_inc(w_split, 1)

            def split_x(t, par):
                dve.tensor_tensor(x_lo[par][:, :, :], hT[:, :, ds(t * P, P)], x_hi[par][:, :, :].bitcast(F32),
                                  ALU.subtract).then_inc(x_split, 1)

            with dve.Fori(0, DC) as i:
                dve.wait_ge(w_hi_ready, 2 * i + 1)
                split_w(0, i, 0)
                dve.wait_ge(w_hi_ready, 2 * i + 2)
                split_w(0, i, 1)
            dve.wait_ge(x_hi_ready, 1)
            split_x(0, 0)

            def rope_tile(h, t, par, G):
                g = h * T + t
                dve.wait_ge(roped, g)
                dve.wait_ge(consumed, G + 2)
                dve.wait_ge(rope_landed[par], 8 * (g - par) + 16)
                dve.wait_ge(qk_stored[par], 8 * (g - par))
                rp, out = rope_in[par], qk_out[par]
                dve.tensor_tensor(out[:, :, :, :].rearrange("p a b d -> p (a b) d"),
                                  qk_dec[:, :, :, :].rearrange("p a b d -> p (a b) d"),
                                  rp[:, 0:1, :].to_broadcast([P, 4, P]), ALU.mult).then_inc(rope_parts, 1)
                dve.tensor_tensor(sin_part[:, :, 0, :], qk_dec[:, :, 1, :],
                                  rp[:, 1:2, :].to_broadcast([P, 2, P]), ALU.mult).then_inc(rope_parts, 1)
                dve.tensor_tensor(sin_part[:, :, 1, :], qk_dec[:, :, 0, :],
                                  rp[:, 2:3, :].to_broadcast([P, 2, P]), ALU.mult).then_inc(rope_parts, 1)
                dve.wait_ge(rope_parts, 3 * (g + 1))
                dve.tensor_tensor(out[:, :, :, :], out[:, :, :, :], sin_part[:, :, :, :], ALU.add).then_inc(roped, 1)

            def retain_tile(h, t, par):
                g = h * T + t
                dve.wait_ge(scored, g + 1)
                dve.wait_ge(mixed, g)
                dve.tensor_tensor(scores[:, :], ps_s[:, 0:P], mask_sb[:, ds(h, 1), :].rearrange("p a n -> p (a n)"),
                                  ALU.mult).then_inc(masked, 1)
                dve.wait_ge(mixed, g + 1)
                dve.bn_stats(stats[:, :], ps_o[:, :]).then_inc(stats_ready, 1)
                dve.wait_ge(stats_ready, g + 1)
                s.passed(dve)
                dve.bn_aggr(mean_var[:, :], stats[:, :]).then_inc(mean_ready, 1)
                dve.wait_ge(outer_ready, g + 1)
                dve.scalar_tensor_tensor(out=state[:, :, :], in0=state[:, :, :], scalar=decay_sb[:, ds(3 * h + 2, 1)],
                                         in1=ps_state[:, :, :], op0=ALU.mult, op1=ALU.add).then_inc(state_ready, 1)
                dve.wait_ge(rstd_ready, g + 1)
                dve.tensor_scalar(normed[:, :], ps_o[:, :], mean_var[:, 0:1], rstd[:, 0:1],
                                  ALU.subtract, ALU.mult).then_inc(normed_ready, 1)
                dve.wait_ge(normed_ready, g + 1)
                dve.wait_ge(gate_landed[par], 8 * (g - par) + 16)
                dve.wait_ge(y_stored[par], 8 * (g - par))
                dve.tensor_tensor(y_out[par][:, :], normed[:, :], gate[par][:, :], ALU.mult).then_inc(y_ready, 1)

            def one_pass(kind, h, p, slot, after):
                if kind == VALUE:
                    dve.memset(state[:, :, :], 0.0).then_inc(state_ready, 1)
                    dve.wait_ge(state_ready, (T + 1) * h + 1)
                    s.passed(dve)

                def tile(t, par, i, more):
                    G = p * T + t
                    dve.wait_ge(x_hi_ready, G + 2)
                    split_x(0 if isinstance(t, int) and t == T - 1 else t + 1, 1 - par)
                    dve.wait_ge(w_hi_ready, G + T + 1)
                    split_w(1 - slot, i, par)
                    if kind == QK:
                        rope_tile(h, t, par, G)
                    elif kind == VALUE:
                        retain_tile(h, t, par)
                over_tiles(dve, tile, lambda j: None)
            passes(dve, one_pass)

        @blk.tensor
        def _(pe):
            def one_pass(kind, h, p, slot, after):
                def tile(t, par, i, more):
                    g, G = h * T + t, p * T + t
                    if kind == VALUE:
                        pe.wait_ge(qk_landed[par], 8 * (g - par) + 16)
                        pe.wait_ge(qkT_ready, g)
                        for a in range(4):
                            last = pe.transpose(ps_t[:, a, :], qk_in[par][:, a, :], ident[:, :])
                        last.then_inc(qk_transposed, 1)
                    pe.wait_ge(x_split, G + 1)
                    pe.wait_ge(consumed, G)
                    for c in range(DC):
                        last = three_pass(pe, ps_p[par][:, :], x_hi[par][:, c, :], x_lo[par][:, c, :],
                                          w_hi[slot][:, c, :], w_lo[slot][:, c, :], c == 0, c == DC - 1)
                    last.then_inc(projected, 1)
                    if kind != VALUE:
                        return
                    pe.wait_ge(qkT_ready, g + 1)
                    pe.wait_ge(masked, g)
                    for j in range(2):
                        last = pe.matmul(ps_s[:, 0:P], qkT[:, 2 + j, :], qkT[:, j, :], start=j == 0, stop=j == 1)
                    last.then_inc(scored, 1)
                    pe.wait_ge(state_ready, (T + 1) * h + t + 1)
                    pe.wait_ge(normed_ready, g)
                    for j in range(2):
                        pe.matmul(ps_o[:, :], qkT[:, j, :], state[:, j, :], start=j == 0, stop=False)
                    pe.wait_ge(masked, g + 1)
                    pe.wait_ge(consumed, G + 2)
                    pe.matmul(ps_o[:, :], scores[:, :], value[:, :], start=False, stop=True).then_inc(mixed, 1)
                    for j in range(2):
                        last = pe.matmul(ps_state[:, j, :], qk_in[par][:, 2 + j, :], value[:, :], start=True, stop=True)
                    last.then_inc(outer_ready, 1)

                pe.wait_ge(w_split, T * (p + 1))
                s.passed(pe)
                over_tiles(pe, tile, lambda j: None)
            passes(pe, one_pass)



class Tail:

    def __init__(self, s, gain, router, bias, x_rows, h_rows, logits, ident):
        self.s, self.gain, self.router, self.bias = s, gain, router, bias
        self.x_rows, self.h_rows, self.logits, self.ident = x_rows, h_rows, logits, ident
        self.xn = s.slots("xn", 2, [P, D])
        self.hn = s.sb("hn", [P, D])
        self.hnT = s.sb("hnT", [P, DC, P])
        self.gain_b = s.sb("gain_b", [P, D])
        self.router_sb = s.sb("router_sb", [P, DC, ROUTES])
        self.bias_b = s.sb("bias_b", [P, ROUTES])
        self.sumsq = s.sb("sumsq", [P, 1])
        self.mean_eps = s.sb("mean_eps", [P, 1])
        self.rstd = s.sb("rstd", [P, 1])
        self.ps_h = s.ps("ps_h", [P, 4, P])
        self.ps_r = s.ps("ps_r", [P, 512])
        self.consts = s.sem("tail_consts")
        self.xn_ready = s.sem("xn_ready")
        self.xn_stored = [s.sem(f"xn_stored{i}") for i in range(2)]
        self.sumsq_ready = s.sem("sumsq_ready")
        self.mean_ready = s.sem("mean_ready")
        self.rstd_ready = s.sem("rstd_ready")
        self.hn_ready = s.sem("hn_ready")
        self.hn_stored = s.sem("hn_stored")
        self.h_transposed = s.sem("h_transposed")
        self.h_copied = s.sem("h_copied")
        self.routed = s.sem("routed")
        self.logits_ready = s.sem("logits_ready")

    def load_consts(self, sp):
        w_group, w_expert = self.router
        b_group, b_expert = self.bias
        sp.dma_start(self.gain_b[:, :], self.gain.rearrange("(a d) -> a d", a=1).to_broadcast([P, D])
                     ).then_inc(self.consts, 16)
        sp.dma_start(self.router_sb[:, :, 0:GROUPS], w_group.rearrange("(c p) g -> p c g", p=P)
                     ).then_inc(self.consts, 16)
        sp.dma_start(self.router_sb[:, :, GROUPS:ROUTES], w_expert.rearrange("(c p) g -> p c g", p=P)
                     ).then_inc(self.consts, 16)
        sp.dma_start(self.bias_b[:, 0:GROUPS], b_group.rearrange("(a g) -> a g", a=1).to_broadcast([P, GROUPS])
                     ).then_inc(self.consts, 16)
        sp.dma_start(self.bias_b[:, GROUPS:ROUTES],
                     b_expert.rearrange("g e -> (g e)").rearrange("(a g) -> a g", a=1).to_broadcast([P, EXPERTS])
                     ).then_inc(self.consts, 16)

    def wait_consts(self, eng):
        eng.wait_ge(self.consts, 80)

    def store_x(self, sp, t, par):
        sp.wait_ge(self.xn_ready, t + 1)
        sp.dma_start(self.x_rows[ds(t * P, P), :], self.xn[par][:, :]).then_inc(self.xn_stored[par], 16)

    def store_h(self, sp, t):
        sp.wait_ge(self.hn_ready, t + 1)
        sp.dma_start(self.h_rows[ds(t * P, P), :], self.hn[:, :]).then_inc(self.hn_stored, 16)

    def drain_stores(self, sp):
        for i in range(2):
            sp.wait_ge(self.xn_stored[i], 8 * TILES)
        sp.wait_ge(self.hn_stored, 16 * TILES)

    def xn_free(self, dve, t, par):
        dve.wait_ge(self.xn_stored[par], 8 * (t - par))
        if not (isinstance(t, int) and t < 2):
            dve.wait_ge(self.hn_ready, t - 1)

    def square(self, act, t, par):
        act.wait_ge(self.xn_ready, t + 1)
        act.wait_ge(self.hn_stored, 16 * t)
        act.wait_ge(self.h_transposed, 2 * t)
        act.activation(self.hn[:, :], self.xn[par][:, :], ACT.Square, accum_out=self.sumsq[:, :]
                       ).then_inc(self.sumsq_ready, 1)

    def invert(self, pool, t, power):
        pool.wait_ge(self.sumsq_ready, t + 1)
        self.s.passed(pool)
        pool.tensor_scalar(self.mean_eps[:, :], self.sumsq[:, :], 1.0 / D, EPS, ALU.mult, ALU.add
                           ).then_inc(self.mean_ready, 1)
        pool.wait_ge(self.mean_ready, t + 1)
        pool.tensor_tensor(self.rstd[:, :], self.mean_eps[:, :], power, ALU.pow).then_inc(self.rstd_ready, 1)

    def norm(self, dve, t, par):
        dve.wait_ge(self.rstd_ready, t + 1)
        dve.scalar_tensor_tensor(out=self.hn[:, :], in0=self.xn[par][:, :], scalar=self.rstd[:, 0:1],
                                 in1=self.gain_b[:, :], op0=ALU.mult, op1=ALU.mult).then_inc(self.hn_ready, 1)

    def transpose_half(self, pe, t, j):
        pe.wait_ge(self.hn_ready, t + 1)
        pe.wait_ge(self.h_copied, 2 * t + j)
        for c in range(4):
            last = pe.transpose(self.ps_h[:, c, :], self.hn[:, (4 * j + c) * P:(4 * j + c + 1) * P], self.ident[:, :])
        last.then_inc(self.h_transposed, 1)

    def copy_half(self, act, t, j):
        act.wait_ge(self.h_transposed, 2 * t + j + 1)
        act.wait_ge(self.routed, t)
        act.activation(self.hnT[:, 4 * j:4 * j + 4, :], self.ps_h[:, :, :], ACT.Copy).then_inc(self.h_copied, 1)

    def route(self, pe, t):
        pe.wait_ge(self.h_copied, 2 * t + 2)
        pe.wait_ge(self.logits_ready, t)
        for c in range(DC):
            last = pe.matmul(self.ps_r[:, 0:ROUTES], self.hnT[:, c, :], self.router_sb[:, c, :],
                             start=c == 0, stop=c == DC - 1)
        last.then_inc(self.routed, 1)

    def keep_logits(self, dve, t):
        dve.wait_ge(self.routed, t + 1)
        self.s.passed(dve)
        dve.tensor_tensor(self.logits[:, ds(t, 1), :].rearrange("p a r -> p (a r)"), self.ps_r[:, 0:ROUTES],
                          self.bias_b[:, :], ALU.add).then_inc(self.logits_ready, 1)


def staggered(eng, step, stages):
    def which(i):
        return [0 <= i - k < TILES for k in range(stages)]
    lead = stages - 1
    n = (TILES - lead - 1) // 2
    for i in range(lead):
        step(i, i % 2, which(i))
    with eng.Fori(0, n) as j:
        step(2 * j + lead, lead % 2, [True] * stages)
        step(2 * j + lead + 1, (lead + 1) % 2, [True] * stages)
    for i in range(lead + 2 * n, TILES + stages - 1):
        step(i, i % 2, which(i))


def output_projection_phase(nc, past, x, y_rows, w_out, gain, router, bias, x_rows, h_rows, logits, ident):
    with Scope(nc, "outp", past) as s:
        tail = Tail(s, gain, router, bias, x_rows, h_rows, logits, ident)
        raw = s.slots("raw", 2, [P, D]) + [xn[:, :] for xn in tail.xn]
        w_hi = s.sb("w_hi", [P, VC, D], F32R)
        w_lo = s.sb("w_lo", [P, VC, D], F32R)
        y_in = s.sb("y_in", [P, VC, P])
        yT_hi = s.slots("yT_hi", 2, [P, VC, P], F32R)
        yT_lo = s.slots("yT_lo", 2, [P, VC, P], F32R)
        x_in = s.sb("x_in", [P, D])
        power = s.sb("power", [P, 1])
        ps_out = [s.ps(f"ps_out{i}", [P, D]) for i in range(2)]
        ps_yt = [s.ps(f"ps_yt{i}", [P, 4, P]) for i in range(2)]

        w_landed = [s.sem(f"w_landed{i}") for i in range(len(raw))]
        w_hi_ready = s.sem("w_hi_ready")
        w_split = s.sem("w_split")
        y_landed = s.sem("y_landed")
        x_landed = s.sem("x_landed")
        y_transposed = s.sem("y_transposed")
        y_hi_ready = s.sem("y_hi_ready")
        y_split = s.sem("y_split")
        out_ready = s.sem("out_ready")
        power_set = s.sem("power_set")
        blk = s.block()
        NG = VC // 4

        @blk.sync
        def _(sp):
            sp.dma_start(y_in[:, :, :].rearrange("p c v -> p (c v)"), y_rows[0:P, :]).then_inc(y_landed, 16)
            for c in range(VC):
                if c >= len(raw):
                    sp.wait_ge(w_split, c - len(raw) + 1)
                sp.dma_start(raw[c % len(raw)], w_out[c * P:(c + 1) * P, :]).then_inc(w_landed[c % len(raw)], 16)
            tail.load_consts(sp)

            def step(i, par, has):
                if has[0] and not (isinstance(i, int) and i == 0):
                    sp.wait_ge(y_transposed, NG * i)
                    sp.dma_start(y_in[:, :, :].rearrange("p c v -> p (c v)"), y_rows[ds(i * P, P), :]
                                 ).then_inc(y_landed, 16)
                if has[1]:
                    t = i - 1
                    if not (isinstance(t, int) and t == 0):
                        sp.wait_ge(tail.xn_ready, t)
                    sp.dma_start(x_in[:, :], x[ds(t * P, P), :]).then_inc(x_landed, 16)
                if has[2]:
                    tail.store_h(sp, i - 2)
                if has[1]:
                    tail.store_x(sp, t, 1 - par)
            staggered(sp, step, 3)
            tail.drain_stores(sp)

        @blk.gpsimd
        def _(pool):
            s.clear_before(pool)
            pool.memset(power[:, :], -0.5).then_inc(power_set, 1)
            pool.wait_ge(power_set, 1)
            with pool.Fori(0, TILES) as t:
                tail.invert(pool, t, power[:, :])

        @blk.scalar
        def _(act):
            def w_parts():
                for c in range(VC):
                    act.wait_ge(w_landed[c % len(raw)], 16 * (c // len(raw) + 1))
                    act.activation(w_hi[:, c, :], raw[c % len(raw)], ACT.Copy).then_inc(w_hi_ready, 1)

            def step(i, par, has):
                for k in range(NG):
                    if has[0]:
                        if k == 0 and not (isinstance(i, int) and i == 0):
                            act.wait_ge(out_ready, i - 1)
                        act.wait_ge(y_transposed, NG * i + k + 1)
                        act.activation(yT_hi[par][:, 4 * k:4 * k + 4, :], ps_yt[k % 2][:, :, :], ACT.Copy
                                       ).then_inc(y_hi_ready, 1)
                    if has[2] and k in (1, 2):
                        tail.copy_half(act, i - 2, k - 1)
                if has[1]:
                    tail.square(act, i - 1, 1 - par)
                if isinstance(i, int) and i == 0:
                    w_parts()
            staggered(act, step, 3)

        @blk.vector
        def _(dve):
            def w_parts():
                for c in range(VC):
                    dve.wait_ge(w_hi_ready, c + 1)
                    dve.tensor_tensor(w_lo[:, c, :], raw[c % len(raw)], w_hi[:, c, :].bitcast(F32),
                                      ALU.subtract).then_inc(w_split, 1)
                dve.wait_ge(w_split, VC)
                tail.wait_consts(dve)

            def step(i, par, has):
                for k in range(NG):
                    if has[0]:
                        dve.wait_ge(y_hi_ready, NG * i + k + 1)
                        c = slice(4 * k, 4 * k + 4)
                        dve.tensor_tensor(yT_lo[par][:, c, :], ps_yt[k % 2][:, :, :], yT_hi[par][:, c, :].bitcast(F32),
                                          ALU.subtract).then_inc(y_split, 1)
                    if has[2] and k == 0:
                        tail.norm(dve, i - 2, par)
                if has[1]:
                    t = i - 1
                    dve.wait_ge(out_ready, t + 1)
                    dve.wait_ge(x_landed, 16 * (t + 1))
                    tail.xn_free(dve, t, 1 - par)
                    dve.tensor_tensor(tail.xn[1 - par][:, :], ps_out[1 - par][:, :], x_in[:, :], ALU.add
                                      ).then_inc(tail.xn_ready, 1)
                if has[2]:
                    tail.keep_logits(dve, i - 2)
                if isinstance(i, int) and i == 0:
                    w_parts()
            staggered(dve, step, 3)

        @blk.tensor
        def _(pe):
            def step(i, par, has):
                if isinstance(i, int) and i == 2:
                    tail.wait_consts(pe)
                for k in range(NG):
                    if has[1]:
                        t, out, q = i - 1, ps_out[1 - par], 1 - par
                        if isinstance(t, int) and t == 0:
                            pe.wait_ge(w_split, 4 * (k + 1))
                        elif k == 0:
                            pe.wait_ge(tail.xn_ready, t - 1)
                        pe.wait_ge(y_split, NG * t + k + 1)
                        for n in range(2):
                            cols = slice(n * (D // 2), (n + 1) * (D // 2))
                            for c in range(4 * k, 4 * k + 4):
                                last = three_pass(pe, out[:, cols], yT_hi[q][:, c, :], yT_lo[q][:, c, :],
                                                  w_hi[:, c, cols], w_lo[:, c, cols], c == 0, c == VC - 1)
                        if k == NG - 1:
                            last.then_inc(out_ready, 1)
                    if has[0]:
                        if k == 0:
                            pe.wait_ge(y_landed, 16 * (i + 1))
                        if not (isinstance(i, int) and i == 0 and k < 2):
                            pe.wait_ge(y_split, NG * i + k - 1)
                        for c in range(4):
                            last = pe.transpose(ps_yt[k % 2][:, c, :], y_in[:, 4 * k + c, :], ident[:, :])
                        last.then_inc(y_transposed, 1)
                    if has[2] and k in (1, 2):
                        tail.transpose_half(pe, i - 2, k - 1)
                if has[2]:
                    tail.route(pe, i - 2)
            staggered(pe, step, 3)



def dispatch_phase(nc, past, tag, logits, consts, weight, row_of_token, token_of_row, block_of_expert):
    T = TILES
    with Scope(nc, tag, past) as s:
        c_upper = s.sb("c_upper", [P, P])
        c_ones = s.sb("c_ones", [P, P])
        c_iota = s.sb("c_iota", [P, P])
        c_token = s.sb("c_token", [P, T])
        c_step = s.sb("c_step", [P, 1, T - 1])
        c_rank = s.sb("c_rank", [P, 1, EXPERTS])
        d4 = s.sb("d4", [P, T, GROUPS])
        e4 = s.sb("e4", [P, T, GROUPS])
        g_one = s.sb("g_one", [P, T, GROUPS])
        g_max = s.sb("g_max", [P, T, 1])
        g_gate = s.sb("g_gate", [P, T, 1])
        best = s.sb("best", [P, T, 1])
        el = s.sb("el", [P, T, EXPERTS])
        work = s.sb("work", [P, T, EXPERTS])
        one = s.slots("one", TOPK, [P, T, EXPERTS])
        top = s.slots("top", TOPK, [P, T, 1])
        ratio = s.sb("ratio", [P, T, 1])
        chosen = s.sb("chosen", [P, T, EXPERTS])
        count = s.sb("count", [P, T, EXPERTS])
        before = s.sb("before", [P, T + 1, EXPERTS])
        over = s.sb("over", [P, EXPERTS, T - 1])
        blocks = s.sb("blocks", [P, EXPERTS, 1])
        ones32 = s.sb("ones32", [P, EXPERTS])
        ends = s.sb("ends", [P, EXPERTS])
        base = s.sb("base", [P, EXPERTS])
        place = s.sb("place", [P, TOPK, T])
        row_f = s.sb("row_f", [P, TOPK, T])
        blk_f = s.sb("blk_f", [P, TOPK, T])
        row_i = s.sb("row_i", [P, TOPK, T], I32)
        blk_i = s.sb("blk_i", [P, TOPK, T], I32)
        row_one = s.slots("row_one", 4, [P, P])
        blk_tok = s.slots("blk_tok", 4, [P, BLOCKS])
        ps_rank = s.ps("ps_rank", [P, T, EXPERTS])
        ps_count = s.ps("ps_count", [P, T, EXPERTS])
        ps_token = s.ps("ps_token", [P, 512])

        consts_landed = s.sem("consts_landed")
        dve_done = s.sem("dve_done")
        shifted = s.sem("shifted")
        exps_ready = s.sem("exps_ready")
        gap_ready = s.sem("gap_ready")
        ratio_ready = s.sem("ratio_ready")
        chosen_ready = s.sem("chosen_ready")
        ranked = s.sem("ranked")
        one_hots = s.sem("one_hots")
        spread = s.sem("spread")
        blk = s.block()

        @blk.sync
        def _(sp):
            for dst, src in ((c_upper[:, :], consts["upper"]), (c_ones[:, :], consts["ones"]),
                             (c_iota[:, :], consts["iota"]), (c_token[:, :], consts["token"]),
                             (c_step[:, 0, :], consts["step"]), (c_rank[:, 0, :], consts["rank"])):
                sp.dma_start(dst, src).then_inc(consts_landed, 16)

        @blk.gpsimd
        def _(pool):
            s.clear_before(pool)

        @blk.scalar
        def _(act):
            act.wait_ge(shifted, 1)
            act.activation(e4[:, :, :], d4[:, :, :], ACT.Exp).then_inc(exps_ready, 1)
            act.wait_ge(gap_ready, 1)
            act.activation(ratio[:, :, :], ratio[:, :, :], ACT.Exp).then_inc(ratio_ready, 1)

        @blk.vector
        def _(dve):
            steps = [0]

            def link(ins):
                steps[0] += 1
                ins.then_inc(dve_done, 1)
                dve.wait_ge(dve_done, steps[0])

            def first_of_max(out, values, peak, rank, n):
                wk = work[:, :, 0:n]
                link(dve.tensor_reduce(peak[:, :, :], values, AX.X, ALU.max))
                link(dve.tensor_tensor(wk, values, peak[:, :, :].to_broadcast([P, T, n]), ALU.is_equal))
                link(dve.tensor_tensor(wk, wk, rank.to_broadcast([P, T, n]), ALU.mult))
                link(dve.tensor_reduce(best[:, :, :], wk, AX.X, ALU.max))
                link(dve.tensor_tensor(out, wk, best[:, :, :].to_broadcast([P, T, n]), ALU.is_equal))

            dve.wait_ge(consts_landed, 96)
            gl, elog = logits[:, :, 0:GROUPS], logits[:, :, GROUPS:ROUTES]
            first_of_max(g_one[:, :, :], gl, g_max, c_rank[:, :, 0:GROUPS], GROUPS)
            dve.tensor_tensor(d4[:, :, :], gl, g_max[:, :, :].to_broadcast([P, T, GROUPS]), ALU.subtract
                              ).then_inc(shifted, 1)
            link(dve.tensor_scalar(g_one[:, :, :], g_one[:, :, :], BIG, -BIG, ALU.mult, ALU.add))
            link(dve.tensor_tensor(
                el[:, :, :].rearrange("p t (g e) -> p t g e", g=GROUPS),
                elog.rearrange("p t (g e) -> p t g e", g=GROUPS),
                g_one[:, :, :].rearrange("p t (g a) -> p t g a", a=1).to_broadcast([P, T, GROUPS, PER_GROUP]),
                ALU.add))
            first_of_max(one[0][:, :, :], el[:, :, :], top[0], c_rank[:, :, :], EXPERTS)
            link(dve.scalar_tensor_tensor(out=el[:, :, :], in0=one[0][:, :, :], scalar=-2 * BIG, in1=el[:, :, :],
                                          op0=ALU.mult, op1=ALU.add))
            first_of_max(one[1][:, :, :], el[:, :, :], top[1], c_rank[:, :, :], EXPERTS)
            dve.tensor_tensor(chosen[:, :, :], one[0][:, :, :], one[1][:, :, :], ALU.add).then_inc(chosen_ready, 1)
            dve.tensor_tensor(ratio[:, :, :], top[1][:, :, :], top[0][:, :, :], ALU.subtract).then_inc(gap_ready, 1)
            dve.wait_ge(exps_ready, 1)
            link(dve.tensor_reduce(g_gate[:, :, :], e4[:, :, :], AX.X, ALU.add))
            dve.wait_ge(ratio_ready, 1)
            link(dve.tensor_scalar(best[:, :, :], ratio[:, :, :], 1.0, None, ALU.add))
            link(dve.tensor_tensor(g_gate[:, :, :], g_gate[:, :, :], best[:, :, :], ALU.mult))
            link(dve.reciprocal(weight[:, 0, :], g_gate[:, :, 0]))
            link(dve.tensor_tensor(weight[:, 1, :], weight[:, 0, :], ratio[:, :, 0], ALU.mult))
            dve.wait_ge(ranked, 1)
            link(dve.tensor_copy(count[:, :, :], ps_count[:, :, :]))
            link(dve.memset(before[:, 0, :], 0.0))
            for t in range(T):
                link(dve.tensor_tensor(before[:, t + 1, :], before[:, t, :], count[:, t, :], ALU.add))
            link(dve.tensor_tensor(over[:, :, :], before[:, T:T + 1, :].rearrange("p a e -> p e a").to_broadcast([P, EXPERTS, T - 1]),
                                   c_step[:, :, :].to_broadcast([P, EXPERTS, T - 1]), ALU.is_gt))
            link(dve.tensor_reduce(blocks[:, :, :], over[:, :, :], AX.X, ALU.add))
            link(dve.tensor_scalar(blocks[:, :, :], blocks[:, :, :], 1.0, None, ALU.add))
            link(dve.memset(ones32[:, :], 1.0))
            link(dve.tensor_tensor_scan(ends[:, :], ones32[:, :], blocks[:, :, 0], 0.0, ALU.mult, ALU.add))
            link(dve.tensor_tensor(base[:, :], ends[:, :], blocks[:, :, 0], ALU.subtract))
            link(dve.memset(block_of_expert[:, 0:1], 0))
            link(dve.tensor_copy(block_of_expert[:, 1:EXPERTS + 1], ends[0:1, :]))
            link(dve.tensor_scalar(base[:, :], base[:, :], float(P), None, ALU.mult))
            link(dve.tensor_tensor(work[:, :, :], before[:, 0:T, :],
                                   base[:, :].rearrange("p (a e) -> p a e", a=1).to_broadcast([P, T, EXPERTS]), ALU.add))
            link(dve.tensor_tensor(work[:, :, :], work[:, :, :], ps_rank[:, :, :], ALU.add))
            for k in range(TOPK):
                link(dve.tensor_tensor(one[k][:, :, :], one[k][:, :, :], work[:, :, :], ALU.mult))
                link(dve.tensor_reduce(place[:, k, :], one[k][:, :, :], AX.X, ALU.add))
            link(dve.tensor_copy(row_of_token[:, :, :], place[:, :, :]))
            link(dve.tensor_scalar(blk_i[:, :, :], row_of_token[:, :, :], 7, None, ALU.logical_shift_right))
            link(dve.tensor_scalar(row_i[:, :, :], row_of_token[:, :, :], P - 1, None, ALU.bitwise_and))
            link(dve.tensor_copy(blk_f[:, :, :], blk_i[:, :, :]))
            link(dve.tensor_copy(row_f[:, :, :], row_i[:, :, :]))

            def one_hot_pair(t, k, par):
                n = 2 * t + k
                if not (isinstance(t, int) and t < 2):
                    dve.wait_ge(spread, n - 3)
                s.passed(dve)
                j = 2 * par + k
                dve.tensor_scalar(row_one[j][:, :], c_iota[:, :],
                                  row_f[:, k, ds(t, 1)], None, ALU.is_equal)
                dve.tensor_scalar(blk_tok[j][:, :], c_iota[:, 0:BLOCKS], blk_f[:, k, ds(t, 1)], c_token[:, ds(t, 1)],
                                  ALU.is_equal, ALU.mult).then_inc(one_hots, 1)

            for t in range(2):
                for k in range(TOPK):
                    one_hot_pair(t, k, t)
            with dve.Fori(1, T // 2) as i:
                for par in range(2):
                    for k in range(TOPK):
                        one_hot_pair(2 * i + par, k, par)
            dve.wait_ge(spread, TOPK * T)
            dve.memset(token_of_row[:, BLOCKS:], 0).then_inc(dve_done, 1)
            dve.tensor_copy(token_of_row[:, 0:BLOCKS], ps_token[:, 0:BLOCKS]).then_inc(dve_done, 1)

        @blk.tensor
        def _(pe):
            pe.wait_ge(consts_landed, 96)
            pe.wait_ge(chosen_ready, 1)
            flat = chosen[:, :, :].rearrange("p t e -> p (t e)")
            pe.matmul(ps_rank[:, :, :].rearrange("p t e -> p (t e)"), c_upper[:, :], flat, start=True, stop=True)
            pe.matmul(ps_count[:, :, :].rearrange("p t e -> p (t e)"), c_ones[:, :], flat, start=True, stop=True
                      ).then_inc(ranked, 1)

            def use_pair(t, k, par, first=False, last=False):
                pe.wait_ge(one_hots, 2 * t + k + 1)
                j = 2 * par + k
                pe.matmul(ps_token[:, 0:BLOCKS], row_one[j][:, :], blk_tok[j][:, :], start=first, stop=last
                          ).then_inc(spread, 1)

            for t in range(2):
                for k in range(TOPK):
                    use_pair(t, k, t, first=(t == 0 and k == 0))
            with pe.Fori(1, T // 2 - 1) as i:
                for par in range(2):
                    for k in range(TOPK):
                        use_pair(2 * i + par, k, par)
            for t in range(T - 2, T):
                for k in range(TOPK):
                    use_pair(t, k, t % 2, last=(t == T - 1 and k == TOPK - 1))



class Combine:

    def __init__(self, s, x_rows, y_rows, weight, row_of_token, gain):
        self.s, self.x_rows, self.y_rows = s, x_rows, y_rows
        self.weight, self.row_of_token, self.gain = weight, row_of_token, gain
        self.x_res = s.slots("x_res", 2, [P, D])
        self.x2 = s.slots("x2_", 2, [P, D])
        self.picked = [s.slots(f"picked{i}", TOPK, [P, D]) for i in range(2)]
        self.index = s.sb("index", [P, TOPK], I32)
        self.gain2_b = s.sb("gain2_b", [P, D])
        self.squares = s.sb("squares", [P, D])
        self.sumsq2 = s.sb("sumsq2", [P, 1])
        self.mean_eps2 = s.sb("mean_eps2", [P, 1])
        self.rstd2 = s.sb("rstd2", [P, 1])
        self.gain_landed = s.sem("gain_landed")
        self.x2_landed = [s.sem(f"x2_landed{i}") for i in range(2)]
        self.index_ready = s.sem("index_ready")
        self.picked_landed = [s.sem(f"picked_landed{i}") for i in range(2)]
        self.half_ready = s.sem("half_ready")
        self.x2_ready = s.sem("x2_ready")
        self.sumsq2_ready = s.sem("sumsq2_ready")
        self.mean2_ready = s.sem("mean2_ready")
        self.rstd2_ready = s.sem("rstd2_ready")

    def load_gain(self, sp):
        sp.dma_start(self.gain2_b[:, :], self.gain.rearrange("(a d) -> a d", a=1).to_broadcast([P, D])
                     ).then_inc(self.gain_landed, 16)

    def load(self, sp, t, par):
        if not (isinstance(t, int) and t < 2):
            sp.wait_ge(self.half_ready, t - 1)
        sp.dma_start(self.x_res[par][:, :], self.x_rows[ds(t * P, P), :]).then_inc(self.x2_landed[par], 16)

    def gather(self, pool, t, par):
        if not (isinstance(t, int) and t == 0):
            pool.wait_ge(self.picked_landed[1 - par], 16 * (t + par))
            if not (isinstance(t, int) and t == 1):
                pool.wait_ge(self.x2_ready, t - 1)
            self.s.passed(pool)
        pool.tensor_copy(self.index[:, :], self.row_of_token[:, :, ds(t, 1)].rearrange("p k a -> p (k a)")
                         ).then_inc(self.index_ready, 1)
        pool.wait_ge(self.index_ready, 1)
        pool.sem_clear(self.index_ready)
        for k in range(TOPK):
            pool.indirect_dma_start(
                out=self.picked[par][k][:, :], out_offset=None, in_=self.y_rows[:, :],
                in_offset=bass.IndirectOffsetOnAxis(ap=self.index[:, k:k + 1], axis=0),
            ).then_inc(self.picked_landed[par], 16)

    def add(self, dve, t, par):
        dve.wait_ge(self.x2_landed[par], 8 * (t - par) + 16)
        dve.wait_ge(self.picked_landed[par], 16 * (t - par) + 32)
        for k in range(TOPK):
            if k:
                dve.wait_ge(self.half_ready, t + 1)
            self.s.passed(dve)
            dve.scalar_tensor_tensor(out=self.x2[par][:, :], in0=self.picked[par][k][:, :],
                                     scalar=self.weight[:, k, ds(t, 1)],
                                     in1=(self.x2 if k else self.x_res)[par][:, :],
                                     op0=ALU.mult, op1=ALU.add).then_inc((self.half_ready, self.x2_ready)[k], 1)

    def square(self, act, t, par):
        act.wait_ge(self.x2_ready, t + 1)
        if not (isinstance(t, int) and t == 0):
            act.wait_ge(self.rstd2_ready, t)
        act.activation(self.squares[:, :], self.x2[par][:, :], ACT.Square, accum_out=self.sumsq2[:, :]
                       ).then_inc(self.sumsq2_ready, 1)

    def invert(self, pool, t, power, used):
        pool.wait_ge(self.sumsq2_ready, t + 1)
        if not (isinstance(t, int) and t == 0):
            pool.wait_ge(used, t)
        self.s.passed(pool)
        pool.tensor_scalar(self.mean_eps2[:, :], self.sumsq2[:, :], 1.0 / D, EPS, ALU.mult, ALU.add
                           ).then_inc(self.mean2_ready, 1)
        pool.wait_ge(self.mean2_ready, t + 1)
        pool.tensor_tensor(self.rstd2[:, :], self.mean_eps2[:, :], power, ALU.pow).then_inc(self.rstd2_ready, 1)

    def norm(self, dve, t, par, out, done):
        dve.wait_ge(self.rstd2_ready, t + 1)
        dve.scalar_tensor_tensor(out=out, in0=self.x2[par][:, :], scalar=self.rstd2[:, 0:1],
                                 in1=self.gain2_b[:, :], op0=ALU.mult, op1=ALU.mult).then_inc(done, 1)


def pool_phase(nc, past, x_in_rows, y_rows, weight, row_of_token, gain_mix, windows, w_pool, scale,
               gain, router, bias, x_rows, h_rows, logits, ident):
    with Scope(nc, "pool", past) as s:
        tail = Tail(s, gain, router, bias, x_rows, h_rows, logits, ident)
        comb = Combine(s, x_in_rows, y_rows, weight, row_of_token, gain_mix)
        band = s.sb("band", [P, 3 * PG, P])
        w_sb = s.sb("w_sb", [P, DC, PGD])
        scale_b = s.sb("scale_b", [P, D])
        hp = s.slots("hp", 2, [P, D])
        pooledT = s.sb("pooledT", [P, DC, P])
        scaled = s.sb("scaled", [P, D])
        power = s.sb("power", [P, 1])
        ps_pt = s.ps("ps_pt", [P, DC, P])
        ps_y = s.ps("ps_y", [P, D])

        consts_landed = s.sem("consts_landed")
        power_set = s.sem("power_set")
        hp_ready = s.sem("hp_ready")
        pooled = s.sem("pooled")
        pooled_copied = s.sem("pooled_copied")
        mixed = s.sem("mixed")
        scaled_ready = s.sem("scaled_ready")
        blk = s.block()

        @blk.sync
        def _(sp):
            comb.load_gain(sp)
            comb.load(sp, 0, 0)
            sp.dma_start(band[:, :, :], windows).then_inc(consts_landed, 16)
            sp.dma_start(w_sb[:, :, :], w_pool.rearrange("g (c p) n -> p (g c) n", p=P)).then_inc(consts_landed, 16)
            sp.dma_start(scale_b[:, :], scale.rearrange("(a d) -> a d", a=1).to_broadcast([P, D])
                         ).then_inc(consts_landed, 16)
            tail.load_consts(sp)

            def step(i, par, has):
                if has[0] and not (isinstance(i, int) and i >= TILES - 1):
                    comb.load(sp, i + 1, 1 - par)
                if has[2]:
                    tail.store_h(sp, i - 2)
                if has[1]:
                    tail.store_x(sp, i - 1, 1 - par)
            staggered(sp, step, 3)
            tail.drain_stores(sp)

        @blk.gpsimd
        def _(pool):
            s.clear_before(pool)
            pool.memset(power[:, :], -0.5).then_inc(power_set, 1)
            pool.wait_ge(power_set, 1)
            comb.gather(pool, 0, 0)

            def step(i, par, has):
                if has[0]:
                    if not (isinstance(i, int) and i >= TILES - 1):
                        comb.gather(pool, i + 1, 1 - par)
                    comb.invert(pool, i, power[:, :], hp_ready)
                if has[1]:
                    tail.invert(pool, i - 1, power[:, :])
            staggered(pool, step, 3)

        @blk.scalar
        def _(act):
            def step(i, par, has):
                if has[0]:
                    comb.square(act, i, par)
                if has[1]:
                    act.wait_ge(pooled, i)
                    if not (isinstance(i, int) and i == 1):
                        act.wait_ge(mixed, i - 1)
                    act.activation(pooledT[:, :, :], ps_pt[:, :, :], ACT.Copy).then_inc(pooled_copied, 1)
                if has[2]:
                    tail.copy_half(act, i - 2, 0)
                    tail.copy_half(act, i - 2, 1)
                if has[1]:
                    tail.square(act, i - 1, 1 - par)
            staggered(act, step, 3)

        @blk.vector
        def _(dve):
            tail.wait_consts(dve)
            dve.wait_ge(consts_landed, 48)
            dve.wait_ge(comb.gain_landed, 16)

            def step(i, par, has):
                if has[0]:
                    if not (isinstance(i, int) and i < 2):
                        dve.wait_ge(tail.xn_ready, i - 1)
                        dve.wait_ge(hp_ready, i - 1)
                    comb.add(dve, i, par)
                if has[2]:
                    tail.norm(dve, i - 2, par)
                if has[0]:
                    if not (isinstance(i, int) and i < 2):
                        dve.wait_ge(pooled, i)
                    comb.norm(dve, i, par, hp[par][:, :], hp_ready)
                if has[1]:
                    t, q = i - 1, 1 - par
                    dve.wait_ge(mixed, t + 1)
                    dve.wait_ge(tail.xn_ready, t)
                    dve.tensor_tensor(scaled[:, :], ps_y[:, :], scale_b[:, :], ALU.mult).then_inc(scaled_ready, 1)
                    dve.wait_ge(scaled_ready, t + 1)
                    tail.xn_free(dve, t, q)
                    dve.tensor_tensor(tail.xn[q][:, :], scaled[:, :], comb.x2[q][:, :], ALU.add
                                      ).then_inc(tail.xn_ready, 1)
                if has[2]:
                    tail.keep_logits(dve, i - 2)
            staggered(dve, step, 3)

        @blk.tensor
        def _(pe):
            tail.wait_consts(pe)
            pe.wait_ge(consts_landed, 48)

            def step(i, par, has):
                if has[1]:
                    t, q = i - 1, 1 - par
                    first = isinstance(t, int) and t == 0
                    pe.wait_ge(hp_ready, t + 1)
                    if not first:
                        pe.wait_ge(pooled_copied, t)
                    for c in range(DC):
                        g, cols = c // (DC // PG), slice(c * P, (c + 1) * P)
                        last = pe.matmul(ps_pt[:, c, :], hp[q][:, cols], band[:, PG + g if first else g, :],
                                         start=True, stop=first)
                        if not first:
                            last = pe.matmul(ps_pt[:, c, :], hp[1 - q][:, cols], band[:, 2 * PG + g, :],
                                             start=False, stop=True)
                    last.then_inc(pooled, 1)
                if has[2]:
                    tail.transpose_half(pe, i - 2, 0)
                    tail.transpose_half(pe, i - 2, 1)
                if has[1]:
                    pe.wait_ge(pooled_copied, t + 1)
                    if not first:
                        pe.wait_ge(scaled_ready, t)
                    for g in range(PG):
                        for j in range(DC // PG):
                            c = g * (DC // PG) + j
                            last = pe.matmul(ps_y[:, g * PGD:(g + 1) * PGD], pooledT[:, c, :], w_sb[:, c, :],
                                             start=j == 0, stop=j == DC // PG - 1)
                    last.then_inc(mixed, 1)
                if has[2]:
                    tail.route(pe, i - 2)
            staggered(pe, step, 3)


def final_phase(nc, past, x_in_rows, y_rows, weight, row_of_token, gain, out):
    with Scope(nc, "final", past) as s:
        comb = Combine(s, x_in_rows, y_rows, weight, row_of_token, gain)
        power = s.sb("power", [P, 1])
        y = s.slots("y", 2, [P, D])
        power_set = s.sem("power_set")
        y_ready = s.sem("y_ready")
        y_stored = [s.sem(f"y_stored{i}") for i in range(2)]
        blk = s.block()

        @blk.sync
        def _(sp):
            comb.load_gain(sp)
            comb.load(sp, 0, 0)

            def step(i, par, has):
                if has[0] and not (isinstance(i, int) and i >= TILES - 1):
                    comb.load(sp, i + 1, 1 - par)
                if has[1]:
                    sp.wait_ge(y_ready, i)
                    sp.dma_start(out[ds((i - 1) * P, P), :], y[1 - par][:, :]).then_inc(y_stored[1 - par], 16)
            staggered(sp, step, 2)
            for i in range(2):
                sp.wait_ge(y_stored[i], 8 * TILES)

        @blk.gpsimd
        def _(pool):
            s.clear_before(pool)
            pool.memset(power[:, :], -0.5).then_inc(power_set, 1)
            pool.wait_ge(power_set, 1)
            comb.gather(pool, 0, 0)

            def step(i, par, has):
                if has[0]:
                    if not (isinstance(i, int) and i >= TILES - 1):
                        comb.gather(pool, i + 1, 1 - par)
                    comb.invert(pool, i, power[:, :], y_ready)
            staggered(pool, step, 2)

        @blk.scalar
        def _(act):
            def step(i, par, has):
                if has[0]:
                    comb.square(act, i, par)
            staggered(act, step, 2)

        @blk.vector
        def _(dve):
            dve.wait_ge(comb.gain_landed, 16)

            def norm(t, par):
                dve.wait_ge(y_stored[par], 8 * (t - par))
                comb.norm(dve, t, par, y[par][:, :], y_ready)

            def step(i, par, has):
                if has[0]:
                    if not (isinstance(i, int) and i < 2):
                        dve.wait_ge(y_ready, i - 1)
                    comb.add(dve, i, par)
                if has[1]:
                    norm(i - 1, 1 - par)
            staggered(dve, step, 2)



def trunk(nc, a, c, out):
    x = a["x"].rearrange("b s d -> (b s) d")
    out = out.rearrange("b s d -> (b s) d")

    def scratch(name, shape):
        return nc.dram_tensor(name, shape, F32).ap()

    qk_rows = scratch("qk_rows", [HEADS * SEQ, 2 * DK])
    gate_rows = scratch("gate_rows", [HEADS * SEQ, DV])
    ret_rows = scratch("ret_rows", [SEQ, VDIM])
    expert_rows = scratch("expert_rows", [BLOCKS * P, D])
    x_rows = [scratch(f"x_rows{i}", [SEQ, D]) for i in range(2)]
    h_rows = [scratch(f"h_rows{i}", [SEQ, D]) for i in range(2)]

    past = []
    with ExitStack() as ctx:
        def sb(name, shape, dt=F32):
            return ctx.enter_context(nc.sbuf_tensor(name, shape, dt))

        ident = sb("ident", [P, P])
        logits = sb("logits", [P, TILES, ROUTES])
        weight = sb("weight", [P, TOPK, TILES])
        row_of_token = sb("row_of_token", [P, TOPK, TILES], I32)
        token_of_row = sb("token_of_row", [P, BLOCKS + 2], I32)
        block_of_expert = sb("block_of_expert", [1, EXPERTS + 1], I32)

        with ExitStack() as head:
            hT = head.enter_context(nc.sbuf_tensor("hT", [P, DC, SEQ], F32))
            norm_transpose_phase(nc, past, x, a["norm_mix"][0], hT, ident, c["ident"])
            retention_phase(nc, past, hT, a["ret_w_in"][0], c["rope"], c["decay"], c["mask"],
                            qk_rows, gate_rows, ret_rows, ident, expert_rows)

        def router(layer):
            return ((a["moe_w_group"][layer], a["moe_w_expert"][layer]),
                    (a["moe_b_group"][layer], a["moe_b_expert"][layer]))

        def experts(layer):
            dispatch_phase(nc, past, f"disp{layer}", logits, c, weight, row_of_token, token_of_row, block_of_expert)
            moe_phase(nc, past, f"moe{layer}", h_rows[layer], a["moe_w_gate"][layer], a["moe_w_up"][layer],
                      a["moe_w_down"][layer], expert_rows, token_of_row, block_of_expert, ident)

        output_projection_phase(nc, past, x, ret_rows, a["ret_w_out"][0], a["norm_ffn"][0], *router(0),
                                x_rows[0], h_rows[0], logits, ident)
        experts(0)
        pool_phase(nc, past, x_rows[0], expert_rows, weight, row_of_token, a["norm_mix"][1], c["band"],
                   a["pool_w"][0], a["pool_scale"][0], a["norm_ffn"][1], *router(1),
                   x_rows[1], h_rows[1], logits, ident)
        experts(1)
        final_phase(nc, past, x_rows[1], expert_rows, weight, row_of_token, a["final_norm"], out)



def tables():
    n = np.arange(P)
    half = DK // 2
    inv_freq = (np.float32(1) / np.float32(ROPE_BASE) ** (np.arange(half, dtype=np.float32) / np.float32(half)))
    angle = np.arange(SEQ, dtype=np.float32)[:, None] * inv_freq.astype(np.float32)[None, :]
    rope = np.concatenate([np.cos(angle), -np.sin(angle), np.sin(angle)], axis=1)

    decay = np.zeros((P, 3 * HEADS))
    mask = np.zeros((P, HEADS, P))
    m, q = n[:, None], n[None, :]
    same = m // CHUNK == q // CHUNK
    seen = m // CHUNK <= q // CHUNK
    for h in range(HEADS):
        g = 1.0 - 2.0 ** (-5 - h)
        decay[:, 3 * h] = g ** (n + 1.0)
        decay[:, 3 * h + 1] = g ** (P - 1.0 - n) * DK ** -0.5
        decay[:, 3 * h + 2] = g ** float(P)
        between = np.where(same, g ** np.abs(q - m).astype(float), g ** (q - m).astype(float)) * seen
        mask[:, h, :] = between / (g ** (q + 1.0) * g ** (P - 1.0 - m))

    band = np.zeros((P, 3 * PG, P))
    for i, w in enumerate(WINDOWS):
        inside = (m <= q) & (m > q - w)
        band[:, i, :] = inside / w - (m == q)
        band[:, PG + i, :] = inside / np.minimum(q + 1, w) - (m == q)
        band[:, 2 * PG + i, :] = (m - P > q - w) / w

    f = lambda v: np.ascontiguousarray(v, dtype=np.float32)
    row = lambda v: f(np.broadcast_to(np.asarray(v)[None, :], (P, len(v))))
    return {
        "ident": f(np.eye(P)), "rope": f(rope), "decay": f(decay), "mask": f(mask), "band": f(band),
        "upper": f(m < q), "ones": f(np.ones((P, P))), "iota": row(np.arange(P)),
        "token": f(n[:, None] + P * np.arange(TILES)[None, :]),
        "step": row(P * np.arange(1, TILES)), "rank": row(np.arange(EXPERTS, 0, -1)),
    }


_INS = ["x", "norm_mix", "norm_ffn", "ret_w_in", "ret_w_out", "pool_w", "pool_scale", "moe_w_group",
        "moe_b_group", "moe_w_expert", "moe_b_expert", "moe_w_gate", "moe_w_up", "moe_w_down", "final_norm"]


def kernel(**inputs):
    import concourse.bacc as bacc
    from concourse.bass_utils import run_bass_kernel_spmd

    nc = bacc.Bacc("TRN2", target_bir_lowering=False, num_devices=1)
    arrays = {}

    def declare(name, array):
        arrays[name] = np.ascontiguousarray(array)
        return nc.dram_tensor(name, arrays[name].shape, mybir.dt.from_np(arrays[name].dtype),
                              kind="ExternalInput").ap()

    a = {n: declare(f"in_{n}", inputs[n]) for n in _INS}
    c = {n: declare(f"table_{n}", v) for n, v in tables().items()}
    out = nc.dram_tensor("out_y", (1, SEQ, D), F32, kind="ExternalOutput").ap()
    trunk(nc, a, c, out)
    r = run_bass_kernel_spmd(nc, [arrays], core_ids=[0])
    return r.results[0]["out_y"]
```

```python
from contextlib import ExitStack

import numpy as np
import concourse.bass as bass
from concourse import mybir

F32 = mybir.dt.float32
F32R = mybir.dt.float32r
I32 = mybir.dt.int32
ALU = mybir.AluOpType
ACT = mybir.ActivationFunctionType
AX = mybir.AxisListType

P = 128
SEQ = 2048
D = 1024
DC = D // P
TILES = SEQ // P
EPS = 1e-6

HEADS = 4
DK = D // HEADS
DV = 2 * DK
VDIM = HEADS * DV
VC = VDIM // P
CHUNK = 64
ROPE_BASE = 10000.0

WINDOWS = (2, 4, 8, 16)
REACH = max(WINDOWS)
PG = len(WINDOWS)
PGD = D // PG

GROUPS = 4
PER_GROUP = 8
EXPERTS = GROUPS * PER_GROUP
TOPK = 2
FF = 256
FC = FF // P
ROUTES = GROUPS + EXPERTS
BLOCKS = SEQ * TOPK // P + EXPERTS
BIG = 1e30


def ds(start, size):
    return bass.ds(start, size)


def three_pass(pe, out, x_hi, x_lo, w_hi, w_lo, first, last):
    pe.matmul(out, x_hi, w_hi, start=first, stop=False)
    pe.matmul(out, x_hi, w_lo, start=False, stop=False)
    return pe.matmul(out, x_lo, w_hi, start=False, stop=last)


def skewed(eng, n, front, back, unroll, depth):
    for t in range(depth):
        front(t, t % unroll)

    def step(t, slot, more=True):
        if more:
            front(t + depth, (slot + depth) % unroll)
        back(t, slot)
    with eng.Fori(0, n // unroll - 1) as i:
        for slot in range(unroll):
            step(unroll * i + slot, slot)
    for slot in range(unroll):
        step(n - unroll + slot, slot, slot < unroll - depth)


class Scope:

    def __init__(self, nc, tag, past):
        self.nc, self.tag, self.ctx, self.ticks = nc, tag, ExitStack(), {}
        self.sems, self.past = [], past

    def __enter__(self):
        self.ctx.__enter__()
        return self

    def __exit__(self, *a):
        self.ctx.__exit__(*a)
        if self.past:
            for sem in self.past[-1].sems:
                self.nc.release_semaphore(sem)
        self.past.append(self)

    def clear_before(self, eng):
        for sem in self.past[-1].sems:
            eng.sem_clear(sem)

    def sb(self, name, shape, dt=F32):
        return self.ctx.enter_context(self.nc.sbuf_tensor(f"{self.tag}_{name}", shape, dt))

    def slots(self, name, n, shape, dt=F32):
        t = self.sb(name, [shape[0], n] + shape[1:], dt)
        return [t[:, i] for i in range(n)]

    def ps(self, name, shape, dt=F32):
        return self.ctx.enter_context(self.nc.psum_tensor(f"{self.tag}_{name}", shape, dt))

    def sem(self, name):
        self.sems.append(self.nc.alloc_semaphore(f"{self.tag}_{name}"))
        return self.sems[-1]

    def passed(self, eng):
        eng.sem_inc(self.ticks[eng.engine], 1)

    def block(self):
        for name in ("PE", "DVE", "Activation", "Pool", "SP"):
            self.ticks[mybir.EngineType[name]] = self.sem(f"passed_{name}")
        return self.ctx.enter_context(self.nc.Block())



def dispatch(s, banks, logits, consts, weight, row_of_token, token_of_row, block_of_expert):
    T = TILES
    c_upper = s.sb("c_upper", [P, P])
    c_ones = s.sb("c_ones", [P, P])
    c_iota = s.sb("c_iota", [P, P])
    c_token = s.sb("c_token", [P, T])
    c_step = s.sb("c_step", [P, 1, T - 1])
    c_rank = s.sb("c_rank", [P, 1, EXPERTS])
    d4 = s.sb("d4", [P, T, GROUPS])
    e4 = s.sb("e4", [P, T, GROUPS])
    g_one = s.sb("g_one", [P, T, GROUPS])
    g_max = s.sb("g_max", [P, T, 1])
    g_gate = s.sb("g_gate", [P, T, 1])
    best = s.sb("best", [P, T, 1])
    el = s.sb("el", [P, T, EXPERTS])
    work = s.sb("work", [P, T, EXPERTS])
    one = s.slots("one", TOPK, [P, T, EXPERTS])
    top = s.slots("top", TOPK, [P, T, 1])
    ratio = s.sb("ratio", [P, T, 1])
    chosen = s.sb("chosen", [P, T, EXPERTS])
    count = s.sb("count", [P, T, EXPERTS])
    before = s.sb("before", [P, T + 1, EXPERTS])
    over = s.sb("over", [P, EXPERTS, T - 1])
    blocks = s.sb("blocks", [P, EXPERTS, 1])
    ones32 = s.sb("ones32", [P, EXPERTS])
    ends = s.sb("ends", [P, EXPERTS])
    base = s.sb("base", [P, EXPERTS])
    place = s.sb("place", [P, TOPK, T])
    row_f = s.sb("row_f", [P, TOPK, T])
    blk_f = s.sb("blk_f", [P, TOPK, T])
    row_i = s.sb("row_i", [P, TOPK, T], I32)
    blk_i = s.sb("blk_i", [P, TOPK, T], I32)
    row_one = s.slots("row_one", 4, [P, P])
    blk_tok = s.slots("blk_tok", 4, [P, BLOCKS])
    ps_rank, ps_count = (b[:, :, :].rearrange("p a (b e) -> p (a b) e", b=P // EXPERTS) for b in banks[0:2])
    ps_token = banks[2]

    consts_landed = s.sem("consts_landed")
    dve_done = s.sem("dve_done")
    shifted = s.sem("shifted")
    exps_ready = s.sem("exps_ready")
    gap_ready = s.sem("gap_ready")
    ratio_ready = s.sem("ratio_ready")
    chosen_ready = s.sem("chosen_ready")
    ranked = s.sem("ranked")
    one_hots = s.sem("one_hots")
    spread = s.sem("spread")
    tables_ready = s.sem("tables_ready")
    def sync(sp):
        for dst, src in ((c_upper[:, :], consts["upper"]), (c_ones[:, :], consts["ones"]),
                         (c_iota[:, :], consts["iota"]), (c_token[:, :], consts["token"]),
                         (c_step[:, 0, :], consts["step"]), (c_rank[:, 0, :], consts["rank"])):
            sp.dma_start(dst, src).then_inc(consts_landed, 16)

    def scalar(act, between=None):
        act.wait_ge(shifted, 1)
        act.activation(e4[:, :, :], d4[:, :, :], ACT.Exp).then_inc(exps_ready, 1)
        between()
        act.wait_ge(gap_ready, 1)
        act.activation(ratio[:, :, :], ratio[:, :, :], ACT.Exp).then_inc(ratio_ready, 1)

    def vector(dve):
        steps = [0]

        def link(ins):
            steps[0] += 1
            ins.then_inc(dve_done, 1)
            dve.wait_ge(dve_done, steps[0])

        def first_of_max(out, values, peak, rank, n):
            wk = work[:, :, 0:n]
            link(dve.tensor_reduce(peak[:, :, :], values, AX.X, ALU.max))
            link(dve.tensor_tensor(wk, values, peak[:, :, :].to_broadcast([P, T, n]), ALU.is_equal))
            link(dve.tensor_tensor(wk, wk, rank.to_broadcast([P, T, n]), ALU.mult))
            link(dve.tensor_reduce(best[:, :, :], wk, AX.X, ALU.max))
            link(dve.tensor_tensor(out, wk, best[:, :, :].to_broadcast([P, T, n]), ALU.is_equal))

        dve.wait_ge(consts_landed, 96)
        gl, elog = logits[:, :, 0:GROUPS], logits[:, :, GROUPS:ROUTES]
        first_of_max(g_one[:, :, :], gl, g_max, c_rank[:, :, 0:GROUPS], GROUPS)
        dve.tensor_tensor(d4[:, :, :], gl, g_max[:, :, :].to_broadcast([P, T, GROUPS]), ALU.subtract
                          ).then_inc(shifted, 1)
        link(dve.tensor_scalar(g_one[:, :, :], g_one[:, :, :], BIG, -BIG, ALU.mult, ALU.add))
        link(dve.tensor_tensor(
            el[:, :, :].rearrange("p t (g e) -> p t g e", g=GROUPS),
            elog.rearrange("p t (g e) -> p t g e", g=GROUPS),
            g_one[:, :, :].rearrange("p t (g a) -> p t g a", a=1).to_broadcast([P, T, GROUPS, PER_GROUP]),
            ALU.add))
        first_of_max(one[0][:, :, :], el[:, :, :], top[0], c_rank[:, :, :], EXPERTS)
        link(dve.scalar_tensor_tensor(out=el[:, :, :], in0=one[0][:, :, :], scalar=-2 * BIG, in1=el[:, :, :],
                                      op0=ALU.mult, op1=ALU.add))
        first_of_max(one[1][:, :, :], el[:, :, :], top[1], c_rank[:, :, :], EXPERTS)
        dve.tensor_tensor(chosen[:, :, :], one[0][:, :, :], one[1][:, :, :], ALU.add).then_inc(chosen_ready, 1)
        dve.tensor_tensor(ratio[:, :, :], top[1][:, :, :], top[0][:, :, :], ALU.subtract).then_inc(gap_ready, 1)
        dve.wait_ge(exps_ready, 1)
        link(dve.tensor_reduce(g_gate[:, :, :], e4[:, :, :], AX.X, ALU.add))
        dve.wait_ge(ratio_ready, 1)
        link(dve.tensor_scalar(best[:, :, :], ratio[:, :, :], 1.0, None, ALU.add))
        link(dve.tensor_tensor(g_gate[:, :, :], g_gate[:, :, :], best[:, :, :], ALU.mult))
        link(dve.reciprocal(weight[:, 0, :], g_gate[:, :, 0]))
        link(dve.tensor_tensor(weight[:, 1, :], weight[:, 0, :], ratio[:, :, 0], ALU.mult))
        dve.wait_ge(ranked, 1)
        link(dve.tensor_copy(count[:, :, :], ps_count[:, :, :]))
        link(dve.memset(before[:, 0, :], 0.0))
        for t in range(T):
            link(dve.tensor_tensor(before[:, t + 1, :], before[:, t, :], count[:, t, :], ALU.add))
        link(dve.tensor_tensor(over[:, :, :], before[:, T:T + 1, :].rearrange("p a e -> p e a").to_broadcast([P, EXPERTS, T - 1]),
                               c_step[:, :, :].to_broadcast([P, EXPERTS, T - 1]), ALU.is_gt))
        link(dve.tensor_reduce(blocks[:, :, :], over[:, :, :], AX.X, ALU.add))
        link(dve.tensor_scalar(blocks[:, :, :], blocks[:, :, :], 1.0, None, ALU.add))
        link(dve.memset(ones32[:, :], 1.0))
        link(dve.tensor_tensor_scan(ends[:, :], ones32[:, :], blocks[:, :, 0], 0.0, ALU.mult, ALU.add))
        link(dve.tensor_tensor(base[:, :], ends[:, :], blocks[:, :, 0], ALU.subtract))
        link(dve.memset(block_of_expert[:, 0:1], 0))
        link(dve.tensor_copy(block_of_expert[:, 1:EXPERTS + 1], ends[0:1, :]))
        link(dve.tensor_scalar(base[:, :], base[:, :], float(P), None, ALU.mult))
        link(dve.tensor_tensor(work[:, :, :], before[:, 0:T, :],
                               base[:, :].rearrange("p (a e) -> p a e", a=1).to_broadcast([P, T, EXPERTS]), ALU.add))
        link(dve.tensor_tensor(work[:, :, :], work[:, :, :], ps_rank[:, :, :], ALU.add))
        for k in range(TOPK):
            link(dve.tensor_tensor(one[k][:, :, :], one[k][:, :, :], work[:, :, :], ALU.mult))
            link(dve.tensor_reduce(place[:, k, :], one[k][:, :, :], AX.X, ALU.add))
        link(dve.tensor_copy(row_of_token[:, :, :], place[:, :, :]))
        link(dve.tensor_scalar(blk_i[:, :, :], row_of_token[:, :, :], 7, None, ALU.logical_shift_right))
        link(dve.tensor_scalar(row_i[:, :, :], row_of_token[:, :, :], P - 1, None, ALU.bitwise_and))
        link(dve.tensor_copy(blk_f[:, :, :], blk_i[:, :, :]))
        link(dve.tensor_copy(row_f[:, :, :], row_i[:, :, :]))

        def one_hot_pair(t, k, par):
            n = 2 * t + k
            if not (isinstance(t, int) and t < 2):
                dve.wait_ge(spread, n - 3)
            s.passed(dve)
            j = 2 * par + k
            dve.tensor_scalar(row_one[j][:, :], c_iota[:, :],
                              row_f[:, k, ds(t, 1)], None, ALU.is_equal)
            dve.tensor_scalar(blk_tok[j][:, :], c_iota[:, 0:BLOCKS], blk_f[:, k, ds(t, 1)], c_token[:, ds(t, 1)],
                              ALU.is_equal, ALU.mult).then_inc(one_hots, 1)

        for t in range(2):
            for k in range(TOPK):
                one_hot_pair(t, k, t)
        with dve.Fori(1, T // 2) as i:
            for par in range(2):
                for k in range(TOPK):
                    one_hot_pair(2 * i + par, k, par)
        dve.wait_ge(spread, TOPK * T)
        dve.memset(token_of_row[:, BLOCKS:], 0).then_inc(tables_ready, 1)
        dve.tensor_copy(token_of_row[:, 0:BLOCKS], ps_token[:, 0:BLOCKS]).then_inc(tables_ready, 1)

    def tensor(pe):
        pe.wait_ge(consts_landed, 96)
        pe.wait_ge(chosen_ready, 1)
        flat = chosen[:, :, :].rearrange("p t e -> p (t e)")
        pe.matmul(ps_rank[:, :, :].rearrange("p t e -> p (t e)"), c_upper[:, :], flat, start=True, stop=True)
        pe.matmul(ps_count[:, :, :].rearrange("p t e -> p (t e)"), c_ones[:, :], flat, start=True, stop=True
                  ).then_inc(ranked, 1)

        def use_pair(t, k, par, first=False, last=False):
            pe.wait_ge(one_hots, 2 * t + k + 1)
            j = 2 * par + k
            pe.matmul(ps_token[:, 0:BLOCKS], row_one[j][:, :], blk_tok[j][:, :], start=first, stop=last
                      ).then_inc(spread, 1)

        for t in range(2):
            for k in range(TOPK):
                use_pair(t, k, t, first=(t == 0 and k == 0))
        with pe.Fori(1, T // 2 - 1) as i:
            for par in range(2):
                for k in range(TOPK):
                    use_pair(2 * i + par, k, par)
        for t in range(T - 2, T):
            for k in range(TOPK):
                use_pair(t, k, t % 2, last=(t == T - 1 and k == TOPK - 1))

    return sync, scalar, vector, tensor, tables_ready



def moe_phase(nc, past, tag, h, w_gate, w_up, w_down, y_rows, ident,
              logits, consts, weight, row_of_token, token_of_row, block_of_expert):
    with Scope(nc, tag, past) as s:
        raw_gate = s.slots("raw_gate", 2, [P, DC, FF])
        raw_up = s.slots("raw_up", 2, [P, DC, FF])
        raw_down = s.slots("raw_down", 2, [P, FC, D])
        gu_hi = s.slots("gu_hi", 2, [P, DC, 2 * FF], F32R)
        gu_lo = s.slots("gu_lo", 2, [P, DC, 2 * FF], F32R)
        dn_hi = s.slots("dn_hi", 2, [P, FC, D], F32R)
        dn_lo = s.slots("dn_lo", 2, [P, FC, D], F32R)
        rows = s.sb("rows", [P, D])
        row_index = s.sb("row_index", [P, 1], I32)
        x_hi = s.sb("x_hi", [P, DC, P], F32R)
        x_lo = s.sb("x_lo", [P, DC, P], F32R)
        silu = s.sb("silu", [P, FC, P])
        hid = s.sb("hid", [P, FC, P])
        hT_hi = s.sb("hT_hi", [P, FC, P], F32R)
        hT_lo = s.sb("hT_lo", [P, FC, P], F32R)
        y = s.sb("y", [P, 2, D])

        ps_x = s.ps("ps_x", [P, DC, P])
        ps_gu = [s.ps(f"ps_gu{j}", [P, 4, P]) for j in range(FC)]
        ps_hT = [s.ps(f"ps_hT{j}", [P, 512]) for j in range(FC)]
        ps_y = s.ps("ps_y", [P, D])

        warm = s.sb("warm", [P, 1])
        ones_set = s.sem("ones_set")
        warmed = s.sem("warmed")
        gate_landed = [s.sem(f"gate_landed{i}") for i in range(2)]
        up_landed = [s.sem(f"up_landed{i}") for i in range(2)]
        down_landed = [s.sem(f"down_landed{i}") for i in range(2)]
        w_hi_ready = s.sem("w_hi_ready")
        gu_split = s.sem("gu_split")
        dn_split = s.sem("dn_split")
        index_ready = s.sem("index_ready")
        rows_landed = s.sem("rows_landed")
        xT_ready = s.sem("xT_ready")
        x_hi_ready = s.sem("x_hi_ready")
        x_split = s.sem("x_split")
        gu_ready = s.sem("gu_ready")
        silu_ready = s.sem("silu_ready")
        hid_ready = s.sem("hid_ready")
        hT_ready = s.sem("hT_ready")
        hT_hi_ready = s.sem("hT_hi_ready")
        hT_split = s.sem("hT_split")
        y_summed = s.sem("y_summed")
        y_left = s.sem("y_left")
        y_right = s.sem("y_right")
        y_stored = s.sem("y_stored")
        y_free = s.sem("y_free")

        dispatch_sync, dispatch_scalar, dispatch_vector, dispatch_tensor, tables_ready = dispatch(
            s, (ps_gu[0], ps_gu[1], ps_hT[0]), logits, consts, weight, row_of_token, token_of_row, block_of_expert)

        def wait_tables(eng):
            eng.wait_ge(tables_ready, 2)
            s.passed(eng)

        CHUNKS = 6

        def chunk(buf, par, k):
            if k < 4:
                half, up = k // 2, k % 2
                c = slice(half * DC // 2, (half + 1) * DC // 2)
                if buf is None:
                    return (raw_up if up else raw_gate)[par][:, c, :]
                return buf[0][par][:, c, up * FF:(up + 1) * FF]
            if buf is None:
                return raw_down[par][:, k - 4, :]
            return buf[1][par][:, k - 4, :]

        HI, LO = (gu_hi, dn_hi), (gu_lo, dn_lo)
        landed = [gate_landed, up_landed, gate_landed, up_landed, down_landed, down_landed]

        def over_blocks(eng, e, first_step, step, ready=None):
            b0 = eng.value_load(block_of_expert[0:1, ds(e, 1)], min_val=0, max_val=BLOCKS - 1)
            b1 = eng.value_load(block_of_expert[0:1, ds(e + 1, 1)], min_val=1, max_val=BLOCKS)
            if ready:
                eng.wait_ge(*ready)
            first_step(b0)
            with eng.If(b1 > b0 + 1):
                with eng.Fori(b0 + 1, b1) as b:
                    step(b)

        def over_experts(eng, body):
            with eng.Fori(0, EXPERTS // 2 - 1) as i:
                body(2 * i, 0, True)
                body(2 * i + 1, 1, True)
            body(EXPERTS - 2, 0, True)
            body(EXPERTS - 1, 1, False)

        blk = s.block()

        @blk.sync
        def _(sp):
            dispatch_sync(sp)

            def load(e, par, wait):
                if wait:
                    sp.wait_ge(gu_split, 4 * (e - 1))
                sp.dma_start(raw_gate[par][:, :, :], w_gate[e].rearrange("(c p) f -> p c f", p=P)
                             ).then_inc(gate_landed[par], 16)
                sp.dma_start(raw_up[par][:, :, :], w_up[e].rearrange("(c p) f -> p c f", p=P)
                             ).then_inc(up_landed[par], 16)
                if wait:
                    sp.wait_ge(dn_split, 2 * (e - 1))
                sp.dma_start(raw_down[par][:, :, :], w_down[e].rearrange("(c p) d -> p c d", p=P)
                             ).then_inc(down_landed[par], 16)
            load(0, 0, False)
            load(1, 1, False)
            with sp.Fori(1, EXPERTS // 2) as i:
                load(2 * i, 0, True)
                load(2 * i + 1, 1, True)

        @blk.gpsimd
        def _(pool):
            pool.memset(warm[:, :], 1.0).then_inc(ones_set, 1)
            s.clear_before(pool)
            def gather(b):
                if not (isinstance(b, int) and b == 0):
                    pool.wait_ge(xT_ready, 2 * b)
                pool.tensor_copy(row_index[:, :], token_of_row[:, ds(b, 1)]).then_inc(index_ready, 1)
                pool.wait_ge(index_ready, 1)
                pool.sem_clear(index_ready)
                pool.indirect_dma_start(
                    out=rows[:, :], out_offset=None, in_=h[:, :],
                    in_offset=bass.IndirectOffsetOnAxis(ap=row_index[:, 0:1], axis=0),
                ).then_inc(rows_landed, 16)

            def split_w(e, par, k):
                pool.wait_ge(w_hi_ready, CHUNKS * e + k + 1)
                pool.tensor_tensor(chunk(LO, par, k), chunk(None, par, k),
                                   chunk(HI, par, k).bitcast(F32), ALU.subtract).then_inc(dn_split if k > 3 else gu_split, 1)

            def split_down(e, par):
                for k in (4, 5):
                    split_w(e, par, k)

            def step(b, fill=lambda: None):
                gather(b + 2)
                fill()
                pool.wait_ge(y_left, b + 1)
                pool.wait_ge(y_right, b + 1)
                pool.wait_ge(y_stored, 16 * b)
                pool.sem_inc(y_free, 1)
                pool.dma_start(y_rows[ds(b * P, P), :], y[:, ds(b % 2, 1), :].rearrange("p a d -> p (a d)")
                               ).then_inc(y_stored, 16)

            for k in range(CHUNKS):
                split_w(0, 0, k)
            wait_tables(pool)
            gather(0)
            gather(1)
            pool.sem_inc(y_free, 1)
            def expert(e, par, more):
                over_blocks(pool, e, lambda b: step(b, (lambda: split_down(e + 1, 1 - par)) if more else lambda: None), step)
            over_experts(pool, expert)
            total = pool.value_load(block_of_expert[0:1, EXPERTS:EXPERTS + 1], min_val=1, max_val=BLOCKS)
            pool.wait_ge(y_stored, 16 * total)
            pool.wait_ge(rows_landed, 16 * (total + 2))

        @blk.scalar
        def _(act):
            def split_w(e, pair, par, k):
                act.wait_ge(landed[k][par], 16 * (pair + 1))
                act.activation(chunk(HI, par, k), chunk(None, par, k), ACT.Copy).then_inc(w_hi_ready, 1)

            def split_x(b, j):
                act.wait_ge(xT_ready, 2 * b + j + 1)
                c = slice(4 * j, 4 * j + 4)
                act.activation(x_hi[:, c, :], ps_x[:, c, :], ACT.Copy).then_inc(x_hi_ready, 1)

            def block(b, fill):
                for j in range(FC):
                    fill(2 * j)
                    fill(2 * j + 1)
                    act.wait_ge(gu_ready, 2 * b + j + 1)
                    act.activation(silu[:, j, :], ps_gu[j][:, 0, :], ACT.Silu).then_inc(silu_ready, 1)
                for j in range(FC):
                    act.wait_ge(hT_ready, 2 * b + j + 1)
                    act.activation(hT_hi[:, j, :], ps_hT[j][:, 0:P], ACT.Copy).then_inc(hT_hi_ready, 1)
                    split_x(b + 1, j)
                for k in range(4, CHUNKS):
                    fill(k)
                act.wait_ge(y_summed, 2 * b + 1)
                act.wait_ge(y_free, b + 1)
                s.passed(act)
                act.activation(y[:, ds(b % 2, 1), 0:D // 2].rearrange("p a d -> p (a d)"), ps_y[:, 0:D // 2], ACT.Copy).then_inc(y_left, 1)

            def expert(e, par, more):
                def first(b):
                    if more:
                        act.wait_ge(y_summed, 2 * b)
                        pair = (e + 1) // 2 if isinstance(e, int) else (e + 1 - (1 - par)) // 2
                        block(b, lambda k: split_w(e + 1, pair, 1 - par, k))
                    else:
                        block(b, lambda k: None)
                over_blocks(act, e, first, lambda b: block(b, lambda k: None))

            dispatch_scalar(act, lambda: [split_w(0, 0, 0, k) for k in range(CHUNKS)])
            act.wait_ge(ones_set, 1)
            act.activation(warm[:, :], warm[:, :], ACT.Silu).then_inc(warmed, 1)
            wait_tables(act)
            for j in range(2):
                split_x(0, j)
            over_experts(act, expert)

        @blk.vector
        def _(dve):
            def split_w(e, par, k):
                dve.wait_ge(w_hi_ready, CHUNKS * e + k + 1)
                dve.tensor_tensor(chunk(LO, par, k), chunk(None, par, k),
                                  chunk(HI, par, k).bitcast(F32), ALU.subtract).then_inc(gu_split, 1)

            def split_x(b, j):
                c = slice(4 * j, 4 * j + 4)
                dve.wait_ge(x_hi_ready, 2 * b + j + 1)
                dve.tensor_tensor(x_lo[:, c, :], ps_x[:, c, :], x_hi[:, c, :].bitcast(F32),
                                  ALU.subtract).then_inc(x_split, 1)

            def block(b, fill):
                for j in range(FC):
                    for k in ((0,), (1, 2))[j]:
                        fill(k)
                    dve.wait_ge(silu_ready, 2 * b + j + 1)
                    dve.tensor_tensor(hid[:, j, :], silu[:, j, :], ps_gu[j][:, 1, :], ALU.mult).then_inc(hid_ready, 1)
                for j in range(FC):
                    dve.wait_ge(hT_hi_ready, 2 * b + j + 1)
                    dve.tensor_tensor(hT_lo[:, j, :], ps_hT[j][:, 0:P], hT_hi[:, j, :].bitcast(F32),
                                      ALU.subtract).then_inc(hT_split, 1)
                    split_x(b + 1, j)
                fill(3)
                dve.wait_ge(y_summed, 2 * b + 2)
                dve.wait_ge(y_free, b + 1)
                s.passed(dve)
                dve.tensor_copy(y[:, ds(b % 2, 1), D // 2:D].rearrange("p a d -> p (a d)"), ps_y[:, D // 2:D]).then_inc(y_right, 1)

            def expert(e, par, more):
                if more:
                    first = lambda b: block(b, lambda k: split_w(e + 1, 1 - par, k))
                else:
                    first = lambda b: block(b, lambda k: None)
                over_blocks(dve, e, first, lambda b: block(b, lambda k: None))

            dispatch_vector(dve)
            wait_tables(dve)
            dve.wait_ge(gu_split, 4)
            for j in range(2):
                split_x(0, j)
            over_experts(dve, expert)

        @blk.tensor
        def _(pe):
            def transpose_rows(b):
                pe.wait_ge(rows_landed, 16 * (b + 1))
                for j in range(2):
                    for c in range(4 * j, 4 * j + 4):
                        last = pe.transpose(ps_x[:, c, :], rows[:, c * P:(c + 1) * P], ident[:, :])
                    last.then_inc(xT_ready, 1)

            def block(e, par, b):
                pe.wait_ge(x_split, 2 * b + 2)
                for j in range(FC):
                    for c in range(DC):
                        units = [w[par][:, c, :].rearrange("p (a j n) -> p j a n", a=2, j=FC)[:, j]
                                 for w in (gu_hi, gu_lo)]
                        last = three_pass(pe, ps_gu[j][:, 0:2, :], x_hi[:, c, :], x_lo[:, c, :],
                                          *units, c == 0, c == DC - 1)
                    last.then_inc(gu_ready, 1)
                for j in range(FC):
                    pe.wait_ge(hid_ready, 2 * b + j + 1)
                    pe.transpose(ps_hT[j][:, 0:P], hid[:, j, :], ident[:, :]).then_inc(hT_ready, 1)
                    if j == 0:
                        transpose_rows(b + 1)
                pe.wait_ge(dn_split, 2 * (e + 1))
                pe.wait_ge(y_left, b)
                pe.wait_ge(y_right, b)
                for c in range(FC):
                    pe.wait_ge(hT_split, 2 * b + c + 1)
                    for n in range(2):
                        cols = slice(n * D // 2, (n + 1) * D // 2)
                        last = three_pass(pe, ps_y[:, cols], hT_hi[:, c, :], hT_lo[:, c, :],
                                          dn_hi[par][:, c, cols], dn_lo[par][:, c, cols], c == 0, c == FC - 1)
                        if c == FC - 1:
                            last.then_inc(y_summed, 1)

            def expert(e, par, more):
                over_blocks(pe, e, lambda b: block(e, par, b), lambda b: block(e, par, b),
                            ready=(gu_split, 4 * (e + 1)))

            dispatch_tensor(pe)
            wait_tables(pe)
            transpose_rows(0)
            over_experts(pe, expert)



def norm_transpose_phase(nc, past, x, gain, hT, ident, ident_table, raw, w_first):
    with Scope(nc, "norm0", past) as s:
        gain_b = s.sb("gain_b", [P, D])
        x_in = s.slots("x_in", 4, [P, D])
        square = s.sb("square", [P, D])
        sumsq = s.slots("sumsq", 4, [P, 1])
        mean_eps = s.slots("mean_eps", 4, [P, 1])
        power = s.sb("power", [P, 1])
        rstd = s.slots("rstd", 4, [P, 1])
        hn = s.slots("hn", 2, [P, D])
        ps_t = [s.ps(f"ps_t{i}", [P, DC, P]) for i in range(2)]

        ident_landed = s.sem("ident_landed")
        raw_landed = s.sem("raw_landed")
        gain_landed = s.sem("gain_landed")
        x_landed = [s.sem(f"x_landed{i}") for i in range(4)]
        power_set = s.sem("power_set")
        sumsq_ready = s.sem("sumsq_ready")
        mean_ready = s.sem("mean_ready")
        rstd_ready = s.sem("rstd_ready")
        hn_ready = s.sem("hn_ready")
        transposed = s.sem("transposed")
        left_copied = s.sem("left_copied")
        right_copied = s.sem("right_copied")
        blk = s.block()
        H = DC // 2

        @blk.sync
        def _(sp):
            def load(t, slot):
                if not isinstance(t, int):
                    sp.wait_ge(hn_ready, t - 3)
                sp.dma_start(x_in[slot][:, :], x[ds(t * P, P), :]).then_inc(x_landed[slot], 16)
            for t in range(4):
                load(t, t)
                if t == 0:
                    sp.dma_start(gain_b[:, :], gain.rearrange("(a d) -> a d", a=1).to_broadcast([P, D])
                                 ).then_inc(gain_landed, 16)
                    sp.dma_start(ident[:, :], ident_table).then_inc(ident_landed, 16)
            with sp.Fori(1, TILES // 4) as i:
                for slot in range(4):
                    load(4 * i + slot, slot)
            for src, cols in w_first:
                sp.dma_start(raw[:, :, cols], src).then_inc(raw_landed, 16)
            sp.wait_ge(raw_landed, 16 * len(w_first))

        @blk.gpsimd
        def _(pool):
            pool.memset(power[:, :], -0.5).then_inc(power_set, 1)
            pool.wait_ge(power_set, 1)

            def step(t, slot):
                pool.wait_ge(sumsq_ready, t + 1)
                s.passed(pool)
                pool.tensor_scalar(mean_eps[slot][:, :], sumsq[slot][:, :], 1.0 / D, EPS,
                                   ALU.mult, ALU.add).then_inc(mean_ready, 1)
                pool.wait_ge(mean_ready, t + 1)
                pool.tensor_tensor(rstd[slot][:, :], mean_eps[slot][:, :], power[:, :],
                                   ALU.pow).then_inc(rstd_ready, 1)
            with pool.Fori(0, TILES // 4) as i:
                for slot in range(4):
                    step(4 * i + slot, slot)

        @blk.scalar
        def _(act):
            def front(t, slot):
                par = slot % 2
                act.wait_ge(x_landed[slot], 4 * (t - slot) + 16)
                act.wait_ge(sumsq_ready, t)
                act.activation(square[:, :], x_in[slot][:, :], ACT.Square,
                               accum_out=sumsq[slot][:, :]).then_inc(sumsq_ready, 1)

            def back(t, slot):
                par = slot % 2
                act.wait_ge(transposed, t + 1)
                s.passed(act)
                act.activation(hT[:, 0:H, ds(t * P, P)], ps_t[par][:, 0:H, :], ACT.Copy).then_inc(left_copied, 1)
            skewed(act, TILES, front, back, 4, 2)

        @blk.vector
        def _(dve):
            dve.wait_ge(gain_landed, 16)

            def front(t, slot):
                par = slot % 2
                dve.wait_ge(rstd_ready, t + 1)
                if not isinstance(t, int) or t >= 2:
                    dve.wait_ge(transposed, t - 1)
                dve.scalar_tensor_tensor(out=hn[par][:, :], in0=x_in[slot][:, :], scalar=rstd[slot][:, 0:1],
                                         in1=gain_b[:, :], op0=ALU.mult, op1=ALU.mult).then_inc(hn_ready, 1)

            def back(t, slot):
                par = slot % 2
                dve.wait_ge(transposed, t + 1)
                dve.tensor_copy(hT[:, H:DC, ds(t * P, P)], ps_t[par][:, H:DC, :]).then_inc(right_copied, 1)
            skewed(dve, TILES, front, back, 4, 1)

        @blk.tensor
        def _(pe):
            def step(t, par):
                pe.wait_ge(hn_ready, t + 1)
                if not isinstance(t, int) or t >= 2:
                    pe.wait_ge(left_copied, t - 1)
                    pe.wait_ge(right_copied, t - 1)
                for c in range(DC):
                    last = pe.transpose(ps_t[par][:, c, :], hn[par][:, c * P:(c + 1) * P], ident[:, :])
                last.then_inc(transposed, 1)
            pe.wait_ge(ident_landed, 16)
            step(0, 0)
            step(1, 1)
            with pe.Fori(1, TILES // 2) as i:
                step(2 * i, 0)
                step(2 * i + 1, 1)


def retention_phase(nc, past, hT, w_in, rope, decay, mask, qk_rows, gate_rows, y_rows, ident, expert_rows, raw):
    with Scope(nc, "ret", past) as s:
        w_hi = s.slots("w_hi", 2, [P, DC, 512], F32R)
        w_lo = s.slots("w_lo", 2, [P, DC, 512], F32R)
        x_hi = s.slots("x_hi", 2, [P, DC, P], F32R)
        x_lo = s.slots("x_lo", 2, [P, DC, P], F32R)
        gate = s.slots("gate", 2, [P, DV])
        rope_in = s.slots("rope_in", 2, [P, 3, P])
        qk_dec = s.sb("qk_dec", [P, 2, 2, P])
        sin_part = s.sb("sin_part", [P, 2, 2, P])
        qk_out = s.slots("qk_out", 2, [P, 2, 2, P])
        qk_in = s.slots("qk_in", 2, [P, 4, P])
        qkT = s.sb("qkT", [P, 4, P])
        k_hi = s.sb("k_hi", [P, 2, P], F32R)
        k_lo = s.sb("k_lo", [P, 2, P], F32R)
        v_hi = s.sb("v_hi", [P, DV], F32R)
        v_lo = s.sb("v_lo", [P, DV], F32R)
        scores = s.sb("scores", [P, P])
        s_hi = s.sb("s_hi", [P, P], F32R)
        s_lo = s.sb("s_lo", [P, P], F32R)
        state = s.sb("state", [P, 2, DV])
        stats = s.sb("stats", [P, 6])
        mean_var = s.sb("mean_var", [P, 2])
        var_eps = s.sb("var_eps", [P, 1])
        power = s.sb("power", [P, 1])
        rstd = s.sb("rstd", [P, 1])
        normed = s.sb("normed", [P, DV])
        y_out = s.slots("y_out", 2, [P, DV])
        decay_sb = s.sb("decay_sb", [P, 3 * HEADS])
        mask_sb = s.sb("mask_sb", [P, HEADS, P])
        zeros = s.sb("zeros", [P, 512])
        warm = s.sb("warm", [P, 1])

        ps_p = [s.ps(f"ps_p{i}", [P, 512]) for i in range(2)]
        ps_t = s.ps("ps_t", [P, 4, P])
        ps_s = s.ps("ps_s", [P, 512])
        ps_o = s.ps("ps_o", [P, DV])
        ps_state = s.ps("ps_state", [P, 2, DV])

        consts_landed = s.sem("consts_landed")
        raw_landed = [s.sem(f"raw_landed{i}") for i in range(2)]
        w_hi_ready = s.sem("w_hi_ready")
        w_split = s.sem("w_split")
        x_hi_ready = s.sem("x_hi_ready")
        x_split = s.sem("x_split")
        projected = s.sem("projected")
        consumed = s.sem("consumed")
        gate_stored = [s.sem(f"gate_stored{i}") for i in range(2)]
        rope_landed = [s.sem(f"rope_landed{i}") for i in range(2)]
        rope_parts = s.sem("rope_parts")
        roped = s.sem("roped")
        qk_stored = [s.sem(f"qk_stored{i}") for i in range(2)]
        qk_landed = [s.sem(f"qk_landed{i}") for i in range(2)]
        gate_landed = [s.sem(f"gate_landed{i}") for i in range(2)]
        qk_transposed = s.sem("qk_transposed")
        qkT_ready = s.sem("qkT_ready")
        scored = s.sem("scored")
        masked = s.sem("masked")
        k_hi_ready = s.sem("k_hi_ready")
        k_split = s.sem("k_split")
        v_split = s.sem("v_split")
        s_hi_ready = s.sem("s_hi_ready")
        s_split = s.sem("s_split")
        mixed = s.sem("mixed")
        outer_ready = s.sem("outer_ready")
        state_ready = s.sem("state_ready")
        stats_ready = s.sem("stats_ready")
        mean_ready = s.sem("mean_ready")
        var_ready = s.sem("var_ready")
        power_set = s.sem("power_set")
        rstd_ready = s.sem("rstd_ready")
        normed_ready = s.sem("normed_ready")
        y_ready = s.sem("y_ready")
        y_stored = [s.sem(f"y_stored{i}") for i in range(2)]
        zeros_set = s.sem("zeros_set")
        zeros_stored = s.sem("zeros_stored")
        blk = s.block()

        T = TILES
        FIRST_SPARE = SEQ * TOPK
        ZR = (BLOCKS * P - FIRST_SPARE) // (HEADS * T)
        QK, GATE, VALUE = KINDS = range(3)
        HB = (T // 2) // 2

        def passes(eng, body):
            with eng.Fori(0, HEADS // 2) as hp:
                for hh in range(2):
                    for kind in KINDS:
                        after = 2 * hp + 1 if hh == 0 else 2 - 2 * hp
                        body(kind, 2 * hp + hh, 6 * hp + 3 * hh + kind, (3 * hh + kind) % 2, after)

        def over_tiles(eng, tile, half):
            with eng.Fori(0, HB) as i:
                tile(2 * i, 0, i, True)
                tile(2 * i + 1, 1, i, True)
            half(0)
            with eng.Fori(HB, T // 2 - 1) as i:
                tile(2 * i, 0, i, True)
                tile(2 * i + 1, 1, i, True)
            tile(T - 2, 0, T // 2 - 1, False)
            tile(T - 1, 1, T // 2 - 1, False)
            half(1)

        @blk.sync
        def _(sp):
            sp.dma_start(decay_sb[:, :], decay).then_inc(consts_landed, 16)
            sp.dma_start(mask_sb[:, :, :], mask).then_inc(consts_landed, 16)

            def load_half(kind, h, j):
                rows = w_in[j * (D // 2):(j + 1) * (D // 2), :].rearrange("(c p) n -> p c n", p=P)
                c = slice(4 * j, 4 * j + 4)
                if kind == QK:
                    sp.dma_start(raw[:, c, 0:DK], rows[:, :, ds(h * DK, DK)]).then_inc(raw_landed[j], 16)
                    sp.dma_start(raw[:, c, DK:2 * DK], rows[:, :, ds(D + h * DK, DK)]).then_inc(raw_landed[j], 16)
                else:
                    base = 2 * D + (VDIM if kind == GATE else 0)
                    sp.dma_start(raw[:, c, :], rows[:, :, ds(base + h * DV, DV)]).then_inc(raw_landed[j], 32)

            def load_rope(t, par, used):
                if used is not None:
                    sp.wait_ge(rope_parts, used)
                sp.dma_start(rope_in[par][:, :, :], rope[ds(t * P, P), :].rearrange("p (a d) -> p a d", a=3)
                             ).then_inc(rope_landed[par], 16)

            sp.wait_ge(zeros_set, 1)
            for j in range(2):
                sp.wait_ge(w_split, 8 * (j + 1))
                load_half(GATE, 0, j)
            load_rope(0, 0, None)
            load_rope(1, 1, None)

            def one_pass(kind, h, p, slot, after):
                def half(j):
                    sp.wait_ge(w_split, T * (p + 1) + 8 * (j + 1))
                    s.passed(sp)
                    load_half((kind + 2) % 3, h if kind == QK else after, j)
                    s.passed(sp)

                def load_qk(t, par):
                    g = h * T + t
                    sp.dma_start(qk_in[par][:, :, :].rearrange("p a d -> p (a d)"),
                                 qk_rows[ds(g * P, P), :]).then_inc(qk_landed[par], 16)

                def load_gate(t, par):
                    g = h * T + t
                    sp.dma_start(gate[par][:, :], gate_rows[ds(g * P, P), :]).then_inc(gate_landed[par], 16)

                def tile(t, par, i, more):
                    g, G = h * T + t, p * T + t
                    if kind == GATE:
                        sp.wait_ge(consumed, G + 2)
                        sp.dma_start(gate_rows[ds(g * P, P), :], gate[par][:, :]).then_inc(gate_stored[par], 16)
                    elif kind == QK:
                        sp.wait_ge(roped, g + 1)
                        sp.dma_start(qk_rows[ds(g * P, P), :], qk_out[par][:, :, :, :].rearrange(
                            "p a b d -> p (a b d)")).then_inc(qk_stored[par], 16)
                        load_rope(t + 2 if more else par, par, 3 * (g + 1))
                    else:
                        sp.wait_ge(y_ready, g + 1)
                        sp.dma_start(y_rows[ds(t * P, P), ds(h * DV, DV)], y_out[par][:, :]).then_inc(y_stored[par], 16)
                        sp.dma_start(expert_rows[ds(FIRST_SPARE + g * ZR, ZR), :].rearrange("r (a n) -> (r a) n", a=2),
                                     zeros[0:2 * ZR, :]).then_inc(zeros_stored, 16)
                        if more:
                            sp.wait_ge(outer_ready, g + 1)
                            load_qk(t + 2, par)
                            load_gate(t + 2, par)

                if kind == GATE:
                    for i in range(2):
                        sp.wait_ge(qk_stored[i], 8 * T * (h + 1))
                    sp.wait_ge(outer_ready, T * h)
                    load_qk(0, 0)
                    load_qk(1, 1)
                if kind == VALUE:
                    for i in range(2):
                        sp.wait_ge(gate_stored[i], 8 * T * (h + 1))
                    s.passed(sp)
                    load_gate(0, 0)
                    load_gate(1, 1)
                over_tiles(sp, tile, half)
            passes(sp, one_pass)
            for i in range(2):
                sp.wait_ge(y_stored[i], 8 * T * HEADS)
                sp.wait_ge(rope_landed[i], 8 * T * HEADS + 16)
                sp.wait_ge(raw_landed[i], 32 * (3 * HEADS + 1))
            sp.wait_ge(zeros_stored, 16 * T * HEADS)

        @blk.gpsimd
        def _(pool):
            s.clear_before(pool)
            pool.memset(zeros[:, :], 0.0).then_inc(zeros_set, 1)
            pool.memset(power[:, :], -0.5).then_inc(power_set, 1)
            pool.wait_ge(power_set, 1)
            with pool.Fori(0, HEADS * T) as g:
                pool.wait_ge(mean_ready, g + 1)
                s.passed(pool)
                pool.tensor_scalar(var_eps[:, :], mean_var[:, 1:2], 1.0, EPS, ALU.mult, ALU.add).then_inc(var_ready, 1)
                pool.wait_ge(var_ready, g + 1)
                pool.tensor_tensor(rstd[:, :], var_eps[:, :], power[:, :], ALU.pow).then_inc(rstd_ready, 1)

        def w_chunk(buf, i, par):
            return buf[:, ds(i, 1), par * 256:(par + 1) * 256]

        @blk.scalar
        def _(act):
            act.wait_ge(power_set, 1)
            act.activation(warm[:, :], power[:, :], ACT.Silu).then_inc(consumed, 1)

            def split_w(slot, i, par):
                act.activation(w_chunk(w_hi[slot], i, par), w_chunk(raw, i, par), ACT.Copy).then_inc(w_hi_ready, 1)

            def split_x(t, par):
                act.activation(x_hi[par][:, :, :], hT[:, :, ds(t * P, P)], ACT.Copy).then_inc(x_hi_ready, 1)

            for i in range(4):
                act.activation(w_hi[0][:, 2 * i:2 * i + 2, :], raw[:, 2 * i:2 * i + 2, :], ACT.Copy
                               ).then_inc(w_hi_ready, T // 4)
            split_x(0, 0)
            act.wait_ge(consts_landed, 32)

            def one_pass(kind, h, p, slot, after):
                def tile(t, par, i, more):
                    g, G = h * T + t, p * T + t
                    act.wait_ge(projected, G)
                    s.passed(act)
                    split_x(0 if isinstance(t, int) and t == T - 1 else t + 1, 1 - par)
                    split_w(1 - slot, i, par)
                    if kind == VALUE:
                        act.wait_ge(qk_transposed, g + 1)
                        act.wait_ge(mixed, g)
                        act.activation(qkT[:, :, :], ps_t[:, :, :], ACT.Copy).then_inc(qkT_ready, 1)
                        act.wait_ge(outer_ready, g)
                        act.wait_ge(qk_landed[par], 8 * (g - par) + 16)
                        act.activation(k_hi[:, :, :], qk_in[par][:, 2:4, :], ACT.Copy).then_inc(k_hi_ready, 1)
                    act.wait_ge(projected, G + 1)
                    if kind == GATE:
                        act.wait_ge(gate_stored[par], 8 * (g - par))
                        act.activation(gate[par][:, :], ps_p[par][:, :], ACT.Silu).then_inc(consumed, 1)
                    elif kind == QK:
                        act.wait_ge(rope_parts, 3 * g)
                        s.passed(act)
                        act.activation(qk_dec[:, 0, :, :].rearrange("p b d -> p (b d)"), ps_p[par][:, 0:DK],
                                       ACT.Copy, scale=decay_sb[:, ds(3 * h, 1)])
                        act.activation(qk_dec[:, 1, :, :].rearrange("p b d -> p (b d)"), ps_p[par][:, DK:2 * DK],
                                       ACT.Copy, scale=decay_sb[:, ds(3 * h + 1, 1)]).then_inc(consumed, 1)
                    else:
                        act.activation(v_hi[:, :], ps_p[par][:, :], ACT.Copy).then_inc(consumed, 1)
                        act.wait_ge(masked, g + 1)
                        act.activation(s_hi[:, :], scores[:, :], ACT.Copy).then_inc(s_hi_ready, 1)

                def half(j):
                    if j == 0:
                        act.wait_ge(raw_landed[1], 32 * (p + 1))

                if kind == GATE:
                    act.wait_ge(y_ready, T * h)
                act.wait_ge(raw_landed[0], 32 * (p + 1))
                over_tiles(act, tile, half)
            passes(act, one_pass)

        @blk.vector
        def _(dve):

            def split_w(slot, i, par):
                dve.tensor_tensor(w_chunk(w_lo[slot], i, par), w_chunk(raw, i, par),
                                  w_chunk(w_hi[slot], i, par).bitcast(F32), ALU.subtract).then_inc(w_split, 1)

            def split_x(t, par):
                dve.tensor_tensor(x_lo[par][:, :, :], hT[:, :, ds(t * P, P)], x_hi[par][:, :, :].bitcast(F32),
                                  ALU.subtract).then_inc(x_split, 1)

            for i in range(4):
                dve.wait_ge(w_hi_ready, T // 4 * (i + 1))
                dve.tensor_tensor(w_lo[0][:, 2 * i:2 * i + 2, :], raw[:, 2 * i:2 * i + 2, :],
                                  w_hi[0][:, 2 * i:2 * i + 2, :].bitcast(F32), ALU.subtract).then_inc(w_split, T // 4)
            dve.wait_ge(x_hi_ready, 1)
            split_x(0, 0)
            dve.wait_ge(consts_landed, 32)

            def rope_tile(h, t, par, G):
                g = h * T + t
                dve.wait_ge(roped, g)
                dve.wait_ge(consumed, G + 2)
                dve.wait_ge(rope_landed[par], 8 * (g - par) + 16)
                dve.wait_ge(qk_stored[par], 8 * (g - par))
                rp, out = rope_in[par], qk_out[par]
                dve.tensor_tensor(out[:, :, :, :].rearrange("p a b d -> p (a b) d"),
                                  qk_dec[:, :, :, :].rearrange("p a b d -> p (a b) d"),
                                  rp[:, 0:1, :].to_broadcast([P, 4, P]), ALU.mult).then_inc(rope_parts, 1)
                dve.tensor_tensor(sin_part[:, :, 0, :], qk_dec[:, :, 1, :],
                                  rp[:, 1:2, :].to_broadcast([P, 2, P]), ALU.mult).then_inc(rope_parts, 1)
                dve.tensor_tensor(sin_part[:, :, 1, :], qk_dec[:, :, 0, :],
                                  rp[:, 2:3, :].to_broadcast([P, 2, P]), ALU.mult).then_inc(rope_parts, 1)
                dve.wait_ge(rope_parts, 3 * (g + 1))
                dve.tensor_tensor(out[:, :, :, :], out[:, :, :, :], sin_part[:, :, :, :], ALU.add).then_inc(roped, 1)

            def retain_tile(h, t, par, G):
                g = h * T + t
                dve.wait_ge(k_hi_ready, g + 1)
                dve.tensor_tensor(k_lo[:, :, :], qk_in[par][:, 2:4, :], k_hi[:, :, :].bitcast(F32),
                                  ALU.subtract).then_inc(k_split, 1)
                dve.wait_ge(scored, g + 1)
                dve.wait_ge(mixed, g)
                dve.tensor_tensor(scores[:, :], ps_s[:, 0:P], mask_sb[:, ds(h, 1), :].rearrange("p a n -> p (a n)"),
                                  ALU.mult).then_inc(masked, 1)
                dve.wait_ge(consumed, G + 2)
                dve.tensor_tensor(v_lo[:, :], ps_p[par][:, :], v_hi[:, :].bitcast(F32), ALU.subtract
                                  ).then_inc(v_split, 1)
                dve.wait_ge(s_hi_ready, g + 1)
                dve.tensor_tensor(s_lo[:, :], scores[:, :], s_hi[:, :].bitcast(F32), ALU.subtract
                                  ).then_inc(s_split, 1)
                dve.wait_ge(mixed, g + 1)
                dve.bn_stats(stats[:, :], ps_o[:, :]).then_inc(stats_ready, 1)
                dve.wait_ge(stats_ready, g + 1)
                s.passed(dve)
                dve.bn_aggr(mean_var[:, :], stats[:, :]).then_inc(mean_ready, 1)
                dve.wait_ge(outer_ready, g + 1)
                dve.scalar_tensor_tensor(out=state[:, :, :], in0=state[:, :, :], scalar=decay_sb[:, ds(3 * h + 2, 1)],
                                         in1=ps_state[:, :, :], op0=ALU.mult, op1=ALU.add).then_inc(state_ready, 1)
                dve.wait_ge(rstd_ready, g + 1)
                dve.tensor_scalar(normed[:, :], ps_o[:, :], mean_var[:, 0:1], rstd[:, 0:1],
                                  ALU.subtract, ALU.mult).then_inc(normed_ready, 1)
                dve.wait_ge(normed_ready, g + 1)
                dve.wait_ge(gate_landed[par], 8 * (g - par) + 16)
                dve.wait_ge(y_stored[par], 8 * (g - par))
                dve.tensor_tensor(y_out[par][:, :], normed[:, :], gate[par][:, :], ALU.mult).then_inc(y_ready, 1)

            def one_pass(kind, h, p, slot, after):
                if kind == VALUE:
                    dve.memset(state[:, :, :], 0.0).then_inc(state_ready, 1)
                    dve.wait_ge(state_ready, (T + 1) * h + 1)
                    s.passed(dve)

                def tile(t, par, i, more):
                    G = p * T + t
                    dve.wait_ge(x_hi_ready, G + 2)
                    split_x(0 if isinstance(t, int) and t == T - 1 else t + 1, 1 - par)
                    dve.wait_ge(w_hi_ready, G + T + 1)
                    split_w(1 - slot, i, par)
                    if kind == QK:
                        rope_tile(h, t, par, G)
                    elif kind == VALUE:
                        retain_tile(h, t, par, G)
                over_tiles(dve, tile, lambda j: None)
            passes(dve, one_pass)

        @blk.tensor
        def _(pe):
            def one_pass(kind, h, p, slot, after):
                def tile(t, par, i, more):
                    g, G = h * T + t, p * T + t
                    if kind == VALUE:
                        pe.wait_ge(qk_landed[par], 8 * (g - par) + 16)
                        pe.wait_ge(qkT_ready, g)
                        for a in range(4):
                            last = pe.transpose(ps_t[:, a, :], qk_in[par][:, a, :], ident[:, :])
                        last.then_inc(qk_transposed, 1)
                    pe.wait_ge(x_split, G + 1)
                    pe.wait_ge(consumed, G)
                    for c in range(DC):
                        last = three_pass(pe, ps_p[par][:, :], x_hi[par][:, c, :], x_lo[par][:, c, :],
                                          w_hi[slot][:, c, :], w_lo[slot][:, c, :], c == 0, c == DC - 1)
                    last.then_inc(projected, 1)
                    if kind != VALUE:
                        return
                    pe.wait_ge(qkT_ready, g + 1)
                    pe.wait_ge(masked, g)
                    for j in range(2):
                        last = pe.matmul(ps_s[:, 0:P], qkT[:, 2 + j, :], qkT[:, j, :], start=j == 0, stop=j == 1)
                    last.then_inc(scored, 1)
                    pe.wait_ge(state_ready, (T + 1) * h + t + 1)
                    pe.wait_ge(normed_ready, g)
                    for j in range(2):
                        pe.matmul(ps_o[:, :], qkT[:, j, :], state[:, j, :], start=j == 0, stop=False)
                    pe.wait_ge(v_split, g + 1)
                    pe.wait_ge(s_split, g + 1)
                    three_pass(pe, ps_o[:, :], s_hi[:, :], s_lo[:, :], v_hi[:, :], v_lo[:, :],
                               False, True).then_inc(mixed, 1)
                    pe.wait_ge(k_split, g + 1)
                    for j in range(2):
                        last = three_pass(pe, ps_state[:, j, :], k_hi[:, j, :], k_lo[:, j, :],
                                          v_hi[:, :], v_lo[:, :], True, True)
                    last.then_inc(outer_ready, 1)

                pe.wait_ge(w_split, T * (p + 1))
                s.passed(pe)
                over_tiles(pe, tile, lambda j: None)
            passes(pe, one_pass)



class Tail:

    def __init__(self, s, gain, router, bias, x_rows, h_rows, logits, ident):
        self.s, self.gain, self.router, self.bias = s, gain, router, bias
        self.x_rows, self.h_rows, self.logits, self.ident = x_rows, h_rows, logits, ident
        self.xn = s.slots("xn", 2, [P, D])
        self.hn = s.sb("hn", [P, D])
        self.hnT = s.sb("hnT", [P, DC, P])
        self.gain_b = s.sb("gain_b", [P, D])
        self.router_sb = s.sb("router_sb", [P, DC, ROUTES])
        self.bias_b = s.sb("bias_b", [P, ROUTES])
        self.sumsq = s.sb("sumsq", [P, 1])
        self.mean_eps = s.sb("mean_eps", [P, 1])
        self.rstd = s.sb("rstd", [P, 1])
        self.ps_h = s.ps("ps_h", [P, 4, P])
        self.ps_r = s.ps("ps_r", [P, 512])
        self.consts = s.sem("tail_consts")
        self.xn_ready = s.sem("xn_ready")
        self.xn_stored = [s.sem(f"xn_stored{i}") for i in range(2)]
        self.sumsq_ready = s.sem("sumsq_ready")
        self.mean_ready = s.sem("mean_ready")
        self.rstd_ready = s.sem("rstd_ready")
        self.hn_ready = s.sem("hn_ready")
        self.hn_stored = s.sem("hn_stored")
        self.h_transposed = s.sem("h_transposed")
        self.h_copied = s.sem("h_copied")
        self.routed = s.sem("routed")
        self.logits_ready = s.sem("logits_ready")

    def load_consts(self, sp):
        w_group, w_expert = self.router
        b_group, b_expert = self.bias
        sp.dma_start(self.gain_b[:, :], self.gain.rearrange("(a d) -> a d", a=1).to_broadcast([P, D])
                     ).then_inc(self.consts, 16)
        sp.dma_start(self.router_sb[:, :, 0:GROUPS], w_group.rearrange("(c p) g -> p c g", p=P)
                     ).then_inc(self.consts, 16)
        sp.dma_start(self.router_sb[:, :, GROUPS:ROUTES], w_expert.rearrange("(c p) g -> p c g", p=P)
                     ).then_inc(self.consts, 16)
        sp.dma_start(self.bias_b[:, 0:GROUPS], b_group.rearrange("(a g) -> a g", a=1).to_broadcast([P, GROUPS])
                     ).then_inc(self.consts, 16)
        sp.dma_start(self.bias_b[:, GROUPS:ROUTES],
                     b_expert.rearrange("g e -> (g e)").rearrange("(a g) -> a g", a=1).to_broadcast([P, EXPERTS])
                     ).then_inc(self.consts, 16)

    def wait_consts(self, eng):
        eng.wait_ge(self.consts, 80)

    def store_x(self, sp, t, par):
        sp.wait_ge(self.xn_ready, t + 1)
        sp.dma_start(self.x_rows[ds(t * P, P), :], self.xn[par][:, :]).then_inc(self.xn_stored[par], 16)

    def store_h(self, sp, t):
        sp.wait_ge(self.hn_ready, t + 1)
        sp.dma_start(self.h_rows[ds(t * P, P), :], self.hn[:, :]).then_inc(self.hn_stored, 16)

    def drain_stores(self, sp):
        for i in range(2):
            sp.wait_ge(self.xn_stored[i], 8 * TILES)
        sp.wait_ge(self.hn_stored, 16 * TILES)

    def xn_free(self, dve, t, par):
        dve.wait_ge(self.xn_stored[par], 8 * (t - par))
        if not (isinstance(t, int) and t < 2):
            dve.wait_ge(self.hn_ready, t - 1)

    def square(self, act, t, par):
        act.wait_ge(self.xn_ready, t + 1)
        act.wait_ge(self.hn_stored, 16 * t)
        act.wait_ge(self.h_transposed, 2 * t)
        act.activation(self.hn[:, :], self.xn[par][:, :], ACT.Square, accum_out=self.sumsq[:, :]
                       ).then_inc(self.sumsq_ready, 1)

    def invert(self, pool, t, power):
        pool.wait_ge(self.sumsq_ready, t + 1)
        self.s.passed(pool)
        pool.tensor_scalar(self.mean_eps[:, :], self.sumsq[:, :], 1.0 / D, EPS, ALU.mult, ALU.add
                           ).then_inc(self.mean_ready, 1)
        pool.wait_ge(self.mean_ready, t + 1)
        pool.tensor_tensor(self.rstd[:, :], self.mean_eps[:, :], power, ALU.pow).then_inc(self.rstd_ready, 1)

    def norm(self, dve, t, par):
        dve.wait_ge(self.rstd_ready, t + 1)
        dve.scalar_tensor_tensor(out=self.hn[:, :], in0=self.xn[par][:, :], scalar=self.rstd[:, 0:1],
                                 in1=self.gain_b[:, :], op0=ALU.mult, op1=ALU.mult).then_inc(self.hn_ready, 1)

    def transpose_half(self, pe, t, j):
        pe.wait_ge(self.hn_ready, t + 1)
        pe.wait_ge(self.h_copied, 2 * t + j)
        for c in range(4):
            last = pe.transpose(self.ps_h[:, c, :], self.hn[:, (4 * j + c) * P:(4 * j + c + 1) * P], self.ident[:, :])
        last.then_inc(self.h_transposed, 1)

    def copy_half(self, act, t, j):
        act.wait_ge(self.h_transposed, 2 * t + j + 1)
        act.wait_ge(self.routed, t)
        act.activation(self.hnT[:, 4 * j:4 * j + 4, :], self.ps_h[:, :, :], ACT.Copy).then_inc(self.h_copied, 1)

    def route(self, pe, t):
        pe.wait_ge(self.h_copied, 2 * t + 2)
        pe.wait_ge(self.logits_ready, t)
        for c in range(DC):
            last = pe.matmul(self.ps_r[:, 0:ROUTES], self.hnT[:, c, :], self.router_sb[:, c, :],
                             start=c == 0, stop=c == DC - 1)
        last.then_inc(self.routed, 1)

    def keep_logits(self, dve, t):
        dve.wait_ge(self.routed, t + 1)
        self.s.passed(dve)
        dve.tensor_tensor(self.logits[:, ds(t, 1), :].rearrange("p a r -> p (a r)"), self.ps_r[:, 0:ROUTES],
                          self.bias_b[:, :], ALU.add).then_inc(self.logits_ready, 1)


def staggered(eng, step, stages):
    def which(i):
        return [0 <= i - k < TILES for k in range(stages)]
    lead = stages - 1
    n = (TILES - lead - 2) // 2
    for i in range(lead):
        step(i, i % 2, which(i))
    with eng.Fori(0, n) as j:
        step(2 * j + lead, lead % 2, [True] * stages)
        step(2 * j + lead + 1, (lead + 1) % 2, [True] * stages)
    for i in range(lead + 2 * n, TILES + stages - 1):
        step(i, i % 2, which(i))


def output_projection_phase(nc, past, x, y_rows, w_out, gain, router, bias, x_rows, h_rows, logits, ident):
    with Scope(nc, "outp", past) as s:
        tail = Tail(s, gain, router, bias, x_rows, h_rows, logits, ident)
        raw = s.slots("raw", 2, [P, D]) + [xn[:, :] for xn in tail.xn]
        w_hi = s.sb("w_hi", [P, VC, D], F32R)
        w_lo = s.sb("w_lo", [P, VC, D], F32R)
        y_in = s.sb("y_in", [P, VC, P])
        yT_hi = s.slots("yT_hi", 2, [P, VC, P], F32R)
        yT_lo = s.slots("yT_lo", 2, [P, VC, P], F32R)
        x_in = s.sb("x_in", [P, D])
        power = s.sb("power", [P, 1])
        ps_out = [s.ps(f"ps_out{i}", [P, D]) for i in range(2)]
        ps_yt = [s.ps(f"ps_yt{i}", [P, 4, P]) for i in range(2)]

        w_landed = [s.sem(f"w_landed{i}") for i in range(len(raw))]
        w_hi_ready = s.sem("w_hi_ready")
        w_split = s.sem("w_split")
        y_landed = [s.sem(f"y_landed{j}") for j in range(2)]
        x_landed = s.sem("x_landed")
        y_transposed = s.sem("y_transposed")
        y_hi_ready = s.sem("y_hi_ready")
        y_split = s.sem("y_split")
        out_ready = s.sem("out_ready")
        power_set = s.sem("power_set")
        blk = s.block()
        NG = VC // 4

        @blk.sync
        def _(sp):
            def load_y(t, j):
                sp.dma_start(y_in[:, j * VC // 2:(j + 1) * VC // 2, :].rearrange("p c v -> p (c v)"),
                             y_rows[ds(t * P, P), j * VDIM // 2:(j + 1) * VDIM // 2]).then_inc(y_landed[j], 16)
            load_y(0, 0)
            load_y(0, 1)
            for c in range(VC):
                if c >= len(raw):
                    sp.wait_ge(w_split, c - len(raw) + 1)
                sp.dma_start(raw[c % len(raw)], w_out[c * P:(c + 1) * P, :]).then_inc(w_landed[c % len(raw)], 16)
            tail.load_consts(sp)

            def step(i, par, has):
                if has[0] and not (isinstance(i, int) and i == 0):
                    sp.wait_ge(y_transposed, NG * i)
                    load_y(i, 1)
                if has[1]:
                    t = i - 1
                    if not (isinstance(t, int) and t == 0):
                        sp.wait_ge(tail.xn_ready, t)
                    sp.dma_start(x_in[:, :], x[ds(t * P, P), :]).then_inc(x_landed, 16)
                if has[2]:
                    tail.store_h(sp, i - 2)
                if has[0] and not (isinstance(i, int) and i >= TILES - 1):
                    sp.wait_ge(y_transposed, NG * i + 2)
                    load_y(i + 1, 0)
                if has[1]:
                    tail.store_x(sp, t, 1 - par)
            staggered(sp, step, 4)
            tail.drain_stores(sp)

        @blk.gpsimd
        def _(pool):
            s.clear_before(pool)
            pool.memset(power[:, :], -0.5).then_inc(power_set, 1)
            pool.wait_ge(power_set, 1)
            with pool.Fori(0, TILES) as t:
                tail.invert(pool, t, power[:, :])

        @blk.scalar
        def _(act):
            def w_parts():
                for c in range(VC):
                    act.wait_ge(w_landed[c % len(raw)], 16 * (c // len(raw) + 1))
                    act.activation(w_hi[:, c, :], raw[c % len(raw)], ACT.Copy).then_inc(w_hi_ready, 1)

            def step(i, par, has):
                for k in range(NG):
                    if has[0]:
                        if k == 0 and not (isinstance(i, int) and i == 0):
                            act.wait_ge(out_ready, i - 1)
                        act.wait_ge(y_transposed, NG * i + k + 1)
                        act.activation(yT_hi[par][:, 4 * k:4 * k + 4, :], ps_yt[k % 2][:, :, :], ACT.Copy
                                       ).then_inc(y_hi_ready, 1)
                    if has[2] and k in (1, 2):
                        tail.copy_half(act, i - 2, k - 1)
                if has[1]:
                    tail.square(act, i - 1, 1 - par)
                if isinstance(i, int) and i == 0:
                    w_parts()
            staggered(act, step, 4)

        @blk.vector
        def _(dve):
            def w_parts():
                for c in range(VC):
                    dve.wait_ge(w_hi_ready, c + 1)
                    dve.tensor_tensor(w_lo[:, c, :], raw[c % len(raw)], w_hi[:, c, :].bitcast(F32),
                                      ALU.subtract).then_inc(w_split, 1)
                dve.wait_ge(w_split, VC)
                tail.wait_consts(dve)

            def step(i, par, has):
                for k in range(NG):
                    if has[0]:
                        dve.wait_ge(y_hi_ready, NG * i + k + 1)
                        c = slice(4 * k, 4 * k + 4)
                        dve.tensor_tensor(yT_lo[par][:, c, :], ps_yt[k % 2][:, :, :], yT_hi[par][:, c, :].bitcast(F32),
                                          ALU.subtract).then_inc(y_split, 1)
                    if has[2] and k == 0:
                        tail.norm(dve, i - 2, par)
                    if has[3] and k == 0:
                        tail.keep_logits(dve, i - 3)
                if has[1]:
                    t = i - 1
                    dve.wait_ge(out_ready, t + 1)
                    dve.wait_ge(x_landed, 16 * (t + 1))
                    tail.xn_free(dve, t, 1 - par)
                    dve.tensor_tensor(tail.xn[1 - par][:, :], ps_out[1 - par][:, :], x_in[:, :], ALU.add
                                      ).then_inc(tail.xn_ready, 1)
                if isinstance(i, int) and i == 0:
                    w_parts()
            staggered(dve, step, 4)

        @blk.tensor
        def _(pe):
            def step(i, par, has):
                if isinstance(i, int) and i == 2:
                    tail.wait_consts(pe)
                for k in range(NG):
                    if has[1]:
                        t, out, q = i - 1, ps_out[1 - par], 1 - par
                        if isinstance(t, int) and t == 0:
                            pe.wait_ge(w_split, 4 * (k + 1))
                        elif k == 0:
                            pe.wait_ge(tail.xn_ready, t - 1)
                        pe.wait_ge(y_split, NG * t + k + 1)
                        for n in range(2):
                            cols = slice(n * (D // 2), (n + 1) * (D // 2))
                            for c in range(4 * k, 4 * k + 4):
                                last = three_pass(pe, out[:, cols], yT_hi[q][:, c, :], yT_lo[q][:, c, :],
                                                  w_hi[:, c, cols], w_lo[:, c, cols], c == 0, c == VC - 1)
                        if k == NG - 1:
                            last.then_inc(out_ready, 1)
                    if has[0]:
                        if k % 2 == 0:
                            pe.wait_ge(y_landed[k // 2], 16 * (i + 1))
                        if not (isinstance(i, int) and i == 0 and k < 2):
                            pe.wait_ge(y_split, NG * i + k - 1)
                        for c in range(4):
                            last = pe.transpose(ps_yt[k % 2][:, c, :], y_in[:, 4 * k + c, :], ident[:, :])
                        last.then_inc(y_transposed, 1)
                    if has[2] and k in (1, 2):
                        tail.transpose_half(pe, i - 2, k - 1)
                if has[2]:
                    tail.route(pe, i - 2)
            staggered(pe, step, 4)



class Combine:

    def __init__(self, s, x_rows, y_rows, weight, row_of_token, gain):
        self.s, self.x_rows, self.y_rows = s, x_rows, y_rows
        self.weight, self.row_of_token, self.gain = weight, row_of_token, gain
        self.x_res = s.slots("x_res", 2, [P, D])
        self.x2 = s.slots("x2_", 2, [P, D])
        self.picked = [s.slots(f"picked{i}", TOPK, [P, D]) for i in range(2)]
        self.index = s.sb("index", [P, TOPK], I32)
        self.gain2_b = s.sb("gain2_b", [P, D])
        self.squares = s.sb("squares", [P, D])
        self.sumsq2 = s.sb("sumsq2", [P, 1])
        self.mean_eps2 = s.sb("mean_eps2", [P, 1])
        self.rstd2 = s.sb("rstd2", [P, 1])
        self.gain_landed = s.sem("gain_landed")
        self.x2_landed = [s.sem(f"x2_landed{i}") for i in range(2)]
        self.index_ready = s.sem("index_ready")
        self.picked_landed = [s.sem(f"picked_landed{i}") for i in range(2)]
        self.half_ready = s.sem("half_ready")
        self.x2_ready = s.sem("x2_ready")
        self.sumsq2_ready = s.sem("sumsq2_ready")
        self.mean2_ready = s.sem("mean2_ready")
        self.rstd2_ready = s.sem("rstd2_ready")

    def load_gain(self, sp):
        sp.dma_start(self.gain2_b[:, :], self.gain.rearrange("(a d) -> a d", a=1).to_broadcast([P, D])
                     ).then_inc(self.gain_landed, 16)

    def load(self, sp, t, par):
        if not (isinstance(t, int) and t < 2):
            sp.wait_ge(self.half_ready, t - 1)
        sp.dma_start(self.x_res[par][:, :], self.x_rows[ds(t * P, P), :]).then_inc(self.x2_landed[par], 16)

    def gather(self, pool, t, par):
        if not (isinstance(t, int) and t == 0):
            pool.wait_ge(self.picked_landed[1 - par], 16 * (t + par))
            if not (isinstance(t, int) and t < 2):
                pool.wait_ge(self.x2_ready, t - 1)
            self.s.passed(pool)
        pool.tensor_copy(self.index[:, :], self.row_of_token[:, :, ds(t, 1)].rearrange("p k a -> p (k a)")
                         ).then_inc(self.index_ready, 1)
        pool.wait_ge(self.index_ready, 1)
        pool.sem_clear(self.index_ready)
        for k in range(TOPK):
            pool.indirect_dma_start(
                out=self.picked[par][k][:, :], out_offset=None, in_=self.y_rows[:, :],
                in_offset=bass.IndirectOffsetOnAxis(ap=self.index[:, k:k + 1], axis=0),
            ).then_inc(self.picked_landed[par], 16)

    def add(self, dve, t, par):
        dve.wait_ge(self.x2_landed[par], 8 * (t - par) + 16)
        dve.wait_ge(self.picked_landed[par], 16 * (t - par) + 32)
        for k in range(TOPK):
            if k:
                dve.wait_ge(self.half_ready, t + 1)
            self.s.passed(dve)
            dve.scalar_tensor_tensor(out=self.x2[par][:, :], in0=self.picked[par][k][:, :],
                                     scalar=self.weight[:, k, ds(t, 1)],
                                     in1=(self.x2 if k else self.x_res)[par][:, :],
                                     op0=ALU.mult, op1=ALU.add).then_inc((self.half_ready, self.x2_ready)[k], 1)

    def square(self, act, t, par):
        act.wait_ge(self.x2_ready, t + 1)
        if not (isinstance(t, int) and t == 0):
            act.wait_ge(self.rstd2_ready, t)
        act.activation(self.squares[:, :], self.x2[par][:, :], ACT.Square, accum_out=self.sumsq2[:, :]
                       ).then_inc(self.sumsq2_ready, 1)

    def invert(self, pool, t, power, used):
        pool.wait_ge(self.sumsq2_ready, t + 1)
        if not (isinstance(t, int) and t == 0):
            pool.wait_ge(used, t)
        self.s.passed(pool)
        pool.tensor_scalar(self.mean_eps2[:, :], self.sumsq2[:, :], 1.0 / D, EPS, ALU.mult, ALU.add
                           ).then_inc(self.mean2_ready, 1)
        pool.wait_ge(self.mean2_ready, t + 1)
        pool.tensor_tensor(self.rstd2[:, :], self.mean_eps2[:, :], power, ALU.pow).then_inc(self.rstd2_ready, 1)

    def norm(self, dve, t, par, out, done):
        dve.wait_ge(self.rstd2_ready, t + 1)
        dve.scalar_tensor_tensor(out=out, in0=self.x2[par][:, :], scalar=self.rstd2[:, 0:1],
                                 in1=self.gain2_b[:, :], op0=ALU.mult, op1=ALU.mult).then_inc(done, 1)


def pool_phase(nc, past, x_in_rows, y_rows, weight, row_of_token, gain_mix, windows, w_pool, scale,
               gain, router, bias, x_rows, h_rows, logits, ident):
    with Scope(nc, "pool", past) as s:
        tail = Tail(s, gain, router, bias, x_rows, h_rows, logits, ident)
        comb = Combine(s, x_in_rows, y_rows, weight, row_of_token, gain_mix)
        band = s.sb("band", [P, 3 * PG, P])
        w_sb = s.sb("w_sb", [P, DC, PGD])
        scale_b = s.sb("scale_b", [P, D])
        hp = s.slots("hp", 2, [P, D])
        pooledT = s.sb("pooledT", [P, DC, P])
        scaled = s.sb("scaled", [P, D])
        power = s.sb("power", [P, 1])
        ps_pt = s.ps("ps_pt", [P, DC, P])
        ps_y = s.ps("ps_y", [P, D])

        consts_landed = s.sem("consts_landed")
        power_set = s.sem("power_set")
        hp_ready = s.sem("hp_ready")
        pooled = s.sem("pooled")
        pooled_copied = s.sem("pooled_copied")
        mixed = s.sem("mixed")
        scaled_ready = s.sem("scaled_ready")
        blk = s.block()

        @blk.sync
        def _(sp):
            comb.load(sp, 0, 0)
            comb.load_gain(sp)
            sp.wait_ge(comb.picked_landed[0], 32)
            sp.dma_start(band[:, :, :], windows).then_inc(consts_landed, 16)
            sp.dma_start(w_sb[:, :, :], w_pool.rearrange("g (c p) n -> p (g c) n", p=P)).then_inc(consts_landed, 16)
            sp.dma_start(scale_b[:, :], scale.rearrange("(a d) -> a d", a=1).to_broadcast([P, D])
                         ).then_inc(consts_landed, 16)
            tail.load_consts(sp)

            def step(i, par, has):
                if has[0] and not (isinstance(i, int) and i >= TILES - 1):
                    comb.load(sp, i + 1, 1 - par)
                if has[2]:
                    tail.store_h(sp, i - 2)
                if has[1]:
                    tail.store_x(sp, i - 1, 1 - par)
            staggered(sp, step, 4)
            tail.drain_stores(sp)

        @blk.gpsimd
        def _(pool):
            s.clear_before(pool)
            pool.memset(power[:, :], -0.5).then_inc(power_set, 1)
            pool.wait_ge(power_set, 1)
            comb.gather(pool, 0, 0)
            comb.gather(pool, 1, 1)

            def step(i, par, has):
                if has[0]:
                    comb.invert(pool, i, power[:, :], hp_ready)
                    if not (isinstance(i, int) and i >= TILES - 2):
                        comb.gather(pool, i + 2, par)
                if has[1]:
                    tail.invert(pool, i - 1, power[:, :])
            staggered(pool, step, 4)

        @blk.scalar
        def _(act):
            def step(i, par, has):
                if has[0]:
                    comb.square(act, i, par)
                if has[1]:
                    act.wait_ge(pooled, i)
                    if not (isinstance(i, int) and i == 1):
                        act.wait_ge(mixed, i - 1)
                    act.activation(pooledT[:, :, :], ps_pt[:, :, :], ACT.Copy).then_inc(pooled_copied, 1)
                if has[2]:
                    tail.copy_half(act, i - 2, 0)
                    tail.copy_half(act, i - 2, 1)
                if has[1]:
                    tail.square(act, i - 1, 1 - par)
            staggered(act, step, 4)

        @blk.vector
        def _(dve):
            dve.wait_ge(comb.gain_landed, 16)

            def step(i, par, has):
                if isinstance(i, int) and i == 1:
                    dve.wait_ge(consts_landed, 48)
                    tail.wait_consts(dve)
                if has[0]:
                    if not (isinstance(i, int) and i < 2):
                        dve.wait_ge(tail.xn_ready, i - 1)
                        dve.wait_ge(hp_ready, i - 1)
                    comb.add(dve, i, par)
                if has[2]:
                    tail.norm(dve, i - 2, par)
                if has[0]:
                    if not (isinstance(i, int) and i < 2):
                        dve.wait_ge(pooled, i)
                    comb.norm(dve, i, par, hp[par][:, :], hp_ready)
                if has[3]:
                    tail.keep_logits(dve, i - 3)
                if has[1]:
                    t, q = i - 1, 1 - par
                    dve.wait_ge(mixed, t + 1)
                    dve.wait_ge(tail.xn_ready, t)
                    dve.tensor_tensor(scaled[:, :], ps_y[:, :], scale_b[:, :], ALU.mult).then_inc(scaled_ready, 1)
                    dve.wait_ge(scaled_ready, t + 1)
                    tail.xn_free(dve, t, q)
                    dve.tensor_tensor(tail.xn[q][:, :], scaled[:, :], comb.x2[q][:, :], ALU.add
                                      ).then_inc(tail.xn_ready, 1)
            staggered(dve, step, 4)

        @blk.tensor
        def _(pe):
            pe.wait_ge(consts_landed, 48)

            def step(i, par, has):
                if isinstance(i, int) and i == 2:
                    tail.wait_consts(pe)
                if has[1]:
                    t, q = i - 1, 1 - par
                    first = isinstance(t, int) and t == 0
                    pe.wait_ge(hp_ready, t + 1)
                    if not first:
                        pe.wait_ge(pooled_copied, t)
                    for c in range(DC):
                        g, cols = c // (DC // PG), slice(c * P, (c + 1) * P)
                        last = pe.matmul(ps_pt[:, c, :], hp[q][:, cols], band[:, PG + g if first else g, :],
                                         start=True, stop=first)
                        if not first:
                            last = pe.matmul(ps_pt[:, c, 0:REACH], hp[1 - q][:, cols], band[:, 2 * PG + g, 0:REACH],
                                             start=False, stop=True)
                    last.then_inc(pooled, 1)
                if has[2]:
                    tail.transpose_half(pe, i - 2, 0)
                if has[1]:
                    pe.wait_ge(pooled_copied, t + 1)
                    if not first:
                        pe.wait_ge(scaled_ready, t)
                    for g in range(PG):
                        for j in range(DC // PG):
                            c = g * (DC // PG) + j
                            last = pe.matmul(ps_y[:, g * PGD:(g + 1) * PGD], pooledT[:, c, :], w_sb[:, c, :],
                                             start=j == 0, stop=j == DC // PG - 1)
                    last.then_inc(mixed, 1)
                if has[2]:
                    tail.transpose_half(pe, i - 2, 1)
                    tail.route(pe, i - 2)
            staggered(pe, step, 4)


def final_phase(nc, past, x_in_rows, y_rows, weight, row_of_token, gain, out):
    with Scope(nc, "final", past) as s:
        comb = Combine(s, x_in_rows, y_rows, weight, row_of_token, gain)
        power = s.sb("power", [P, 1])
        y = s.slots("y", 2, [P, D])
        power_set = s.sem("power_set")
        y_ready = s.sem("y_ready")
        y_stored = [s.sem(f"y_stored{i}") for i in range(2)]
        blk = s.block()

        @blk.sync
        def _(sp):
            comb.load_gain(sp)
            comb.load(sp, 0, 0)

            def step(i, par, has):
                if has[0] and not (isinstance(i, int) and i >= TILES - 1):
                    comb.load(sp, i + 1, 1 - par)
                if has[1]:
                    sp.wait_ge(y_ready, i)
                    sp.dma_start(out[ds((i - 1) * P, P), :], y[1 - par][:, :]).then_inc(y_stored[1 - par], 16)
            staggered(sp, step, 2)
            for i in range(2):
                sp.wait_ge(y_stored[i], 8 * TILES)

        @blk.gpsimd
        def _(pool):
            s.clear_before(pool)
            pool.memset(power[:, :], -0.5).then_inc(power_set, 1)
            pool.wait_ge(power_set, 1)
            comb.gather(pool, 0, 0)
            comb.gather(pool, 1, 1)

            def step(i, par, has):
                if has[0]:
                    comb.invert(pool, i, power[:, :], y_ready)
                    if not (isinstance(i, int) and i >= TILES - 2):
                        comb.gather(pool, i + 2, par)
            staggered(pool, step, 2)

        @blk.scalar
        def _(act):
            def step(i, par, has):
                if has[0]:
                    comb.square(act, i, par)
            staggered(act, step, 2)

        @blk.vector
        def _(dve):
            dve.wait_ge(comb.gain_landed, 16)

            def norm(t, par):
                dve.wait_ge(y_stored[par], 8 * (t - par))
                comb.norm(dve, t, par, y[par][:, :], y_ready)

            def step(i, par, has):
                if has[0]:
                    if not (isinstance(i, int) and i < 2):
                        dve.wait_ge(y_ready, i - 1)
                    comb.add(dve, i, par)
                if has[1]:
                    norm(i - 1, 1 - par)
            staggered(dve, step, 2)



def trunk(nc, a, c, out):
    x = a["x"].rearrange("b s d -> (b s) d")
    out = out.rearrange("b s d -> (b s) d")

    def scratch(name, shape):
        return nc.dram_tensor(name, shape, F32).ap()

    qk_rows = scratch("qk_rows", [HEADS * SEQ, 2 * DK])
    gate_rows = scratch("gate_rows", [HEADS * SEQ, DV])
    ret_rows = scratch("ret_rows", [SEQ, VDIM])
    expert_rows = scratch("expert_rows", [BLOCKS * P, D])
    x_rows = [scratch(f"x_rows{i}", [SEQ, D]) for i in range(2)]
    h_rows = [scratch(f"h_rows{i}", [SEQ, D]) for i in range(2)]

    past = []
    with ExitStack() as ctx:
        def sb(name, shape, dt=F32):
            return ctx.enter_context(nc.sbuf_tensor(name, shape, dt))

        ident = sb("ident", [P, P])
        logits = sb("logits", [P, TILES, ROUTES])
        weight = sb("weight", [P, TOPK, TILES])
        row_of_token = sb("row_of_token", [P, TOPK, TILES], I32)
        token_of_row = sb("token_of_row", [P, BLOCKS + 2], I32)
        block_of_expert = sb("block_of_expert", [1, EXPERTS + 1], I32)

        with ExitStack() as head:
            hT = head.enter_context(nc.sbuf_tensor("hT", [P, DC, SEQ], F32))
            raw = head.enter_context(nc.sbuf_tensor("raw", [P, DC, 2 * DK], F32))
            w_rows = a["ret_w_in"][0].rearrange("(c p) n -> p c n", p=P)
            qk_first = [(w_rows[:, :, i * D:i * D + DK], slice(i * DK, (i + 1) * DK)) for i in range(2)]
            norm_transpose_phase(nc, past, x, a["norm_mix"][0], hT, ident, c["ident"], raw, qk_first)
            retention_phase(nc, past, hT, a["ret_w_in"][0], c["rope"], c["decay"], c["mask"],
                            qk_rows, gate_rows, ret_rows, ident, expert_rows, raw)

        def router(layer):
            return ((a["moe_w_group"][layer], a["moe_w_expert"][layer]),
                    (a["moe_b_group"][layer], a["moe_b_expert"][layer]))

        def experts(layer):
            moe_phase(nc, past, f"moe{layer}", h_rows[layer], a["moe_w_gate"][layer], a["moe_w_up"][layer],
                      a["moe_w_down"][layer], expert_rows, ident,
                      logits, c, weight, row_of_token, token_of_row, block_of_expert)

        output_projection_phase(nc, past, x, ret_rows, a["ret_w_out"][0], a["norm_ffn"][0], *router(0),
                                x_rows[0], h_rows[0], logits, ident)
        experts(0)
        pool_phase(nc, past, x_rows[0], expert_rows, weight, row_of_token, a["norm_mix"][1], c["band"],
                   a["pool_w"][0], a["pool_scale"][0], a["norm_ffn"][1], *router(1),
                   x_rows[1], h_rows[1], logits, ident)
        experts(1)
        final_phase(nc, past, x_rows[1], expert_rows, weight, row_of_token, a["final_norm"], out)



def tables():
    n = np.arange(P)
    half = DK // 2
    inv_freq = (np.float32(1) / np.float32(ROPE_BASE) ** (np.arange(half, dtype=np.float32) / np.float32(half)))
    angle = np.arange(SEQ, dtype=np.float32)[:, None] * inv_freq.astype(np.float32)[None, :]
    rope = np.concatenate([np.cos(angle), -np.sin(angle), np.sin(angle)], axis=1)

    decay = np.zeros((P, 3 * HEADS))
    mask = np.zeros((P, HEADS, P))
    m, q = n[:, None], n[None, :]
    same = m // CHUNK == q // CHUNK
    seen = m // CHUNK <= q // CHUNK
    for h in range(HEADS):
        g = 1.0 - 2.0 ** (-5 - h)
        decay[:, 3 * h] = g ** (n + 1.0)
        decay[:, 3 * h + 1] = g ** (P - 1.0 - n) * DK ** -0.5
        decay[:, 3 * h + 2] = g ** float(P)
        between = np.where(same, g ** np.abs(q - m).astype(float), g ** (q - m).astype(float)) * seen
        mask[:, h, :] = between / (g ** (q + 1.0) * g ** (P - 1.0 - m))

    band = np.zeros((P, 3 * PG, P))
    for i, w in enumerate(WINDOWS):
        inside = (m <= q) & (m > q - w)
        band[:, i, :] = inside / w - (m == q)
        band[:, PG + i, :] = inside / np.minimum(q + 1, w) - (m == q)
        band[:, 2 * PG + i, :] = (m - P > q - w) / w

    f = lambda v: np.ascontiguousarray(v, dtype=np.float32)
    row = lambda v: f(np.broadcast_to(np.asarray(v)[None, :], (P, len(v))))
    return {
        "ident": f(np.eye(P)), "rope": f(rope), "decay": f(decay), "mask": f(mask), "band": f(band),
        "upper": f(m < q), "ones": f(np.ones((P, P))), "iota": row(np.arange(P)),
        "token": f(n[:, None] + P * np.arange(TILES)[None, :]),
        "step": row(P * np.arange(1, TILES)), "rank": row(np.arange(EXPERTS, 0, -1)),
    }


_INS = ["x", "norm_mix", "norm_ffn", "ret_w_in", "ret_w_out", "pool_w", "pool_scale", "moe_w_group",
        "moe_b_group", "moe_w_expert", "moe_b_expert", "moe_w_gate", "moe_w_up", "moe_w_down", "final_norm"]


def kernel(**inputs):
    import concourse.bacc as bacc
    from concourse.bass_utils import run_bass_kernel_spmd

    nc = bacc.Bacc("TRN2", target_bir_lowering=False, num_devices=1)
    arrays = {}

    def declare(name, array):
        arrays[name] = np.ascontiguousarray(array)
        return nc.dram_tensor(name, arrays[name].shape, mybir.dt.from_np(arrays[name].dtype),
                              kind="ExternalInput").ap()

    a = {n: declare(f"in_{n}", inputs[n]) for n in _INS}
    c = {n: declare(f"table_{n}", v) for n, v in tables().items()}
    out = nc.dram_tensor("out_y", (1, SEQ, D), F32, kind="ExternalOutput").ap()
    trunk(nc, a, c, out)
    r = run_bass_kernel_spmd(nc, [arrays], core_ids=[0])
    return r.results[0]["out_y"]
```
